# Optimizing a Trainium2 kernel written in Bass

```python
import math
import jax, jax.numpy as jnp
from jax import lax
import numpy as np

D_MODEL = 1024
BATCH = 1
SEQ = 256
DEPTH = 1

HEAD_DIM = 64
N_HEADS_MIX = D_MODEL // HEAD_DIM
N_FOX = N_HEADS_MIX // 2
N_MOBA = N_HEADS_MIX - N_FOX
FOX_W = N_FOX * HEAD_DIM
MOBA_W = N_MOBA * HEAD_DIM
IN_COLS = 3 * FOX_W + N_FOX + 3 * MOBA_W
FOX_Q_BLOCK = 128
MOBA_BLOCK = 256
MOBA_TOPK = 3
MOBA_Q_CHUNK = 16
N_BUCKETS = 32
MAX_DISTANCE = 128
N_MEM = 256
N_CROSS_HEADS = 4
CROSS_HEAD_DIM = D_MODEL // N_CROSS_HEADS
N_EXPERTS = 32
TOP_K = 4
D_EXPERT = D_MODEL
SWIGLU_LIMIT = 7.0
SWIGLU_ALPHA = 1.702
EXPERT_BLOCK = 128
DEEPNORM_ALPHA = (2 * DEPTH) ** 0.25
DEEPNORM_BETA = (8 * DEPTH) ** -0.25
LN_EPS = 1e-5

kernel_name = "fox_moba_hymba_deepnorm_moe"

def layer_norm(x, g, b):
    x32 = x.astype(jnp.float32)
    mu = jnp.mean(x32, axis=-1, keepdims=True)
    var = jnp.mean(jnp.square(x32 - mu), axis=-1, keepdims=True)
    y = (x32 - mu) * lax.rsqrt(var + LN_EPS)
    return (y * g.astype(jnp.float32) + b.astype(jnp.float32)).astype(x.dtype)

def split_heads(t, n_heads, head_dim):
    B, S, _ = t.shape
    return t.reshape(B, S, n_heads, head_dim).transpose(0, 2, 1, 3)

def merge_heads(t):
    B, H, S, d = t.shape
    return t.transpose(0, 2, 1, 3).reshape(B, S, H * d)

def t5_bucket(dist):
    max_exact = N_BUCKETS // 2
    n = jnp.maximum(dist, 0)
    nf = jnp.maximum(n, 1).astype(jnp.float32)
    large = max_exact + (jnp.log(nf / max_exact) / math.log(MAX_DISTANCE / max_exact)
                         * (N_BUCKETS - max_exact)).astype(jnp.int32)
    large = jnp.minimum(large, N_BUCKETS - 1)
    return jnp.where(n < max_exact, n, large)

def fox_attention(q, k, v, log_f):
    B, H, S, d = q.shape
    c = jnp.cumsum(log_f, axis=-1)
    scale = d ** -0.5
    kpos = jnp.arange(S)

    def block(i):
        start = i * FOX_Q_BLOCK
        qb = lax.dynamic_slice_in_dim(q, start, FOX_Q_BLOCK, axis=2)
        cb = lax.dynamic_slice_in_dim(c, start, FOX_Q_BLOCK, axis=2)
        qpos = start + jnp.arange(FOX_Q_BLOCK)
        logits = jnp.einsum('bhqd,bhkd->bhqk', qb, k,
                            preferred_element_type=jnp.float32) * scale
        logits = logits + cb[..., :, None] - c[..., None, :]
        logits = jnp.where(kpos[None, :] <= qpos[:, None], logits, -jnp.inf)
        p = jax.nn.softmax(logits, axis=-1)
        return jnp.einsum('bhqk,bhkd->bhqd', p.astype(v.dtype), v)

    out = lax.map(block, jnp.arange(S // FOX_Q_BLOCK))
    return jnp.moveaxis(out, 0, 2).reshape(B, H, S, d)

def moba_attention(q, k, v, rel_bias):
    B, H, S, d = q.shape
    nblk = -(-S // MOBA_BLOCK)
    pad = nblk * MOBA_BLOCK - S
    kp = jnp.pad(k, ((0, 0), (0, 0), (0, pad), (0, 0)))
    vp = jnp.pad(v, ((0, 0), (0, 0), (0, pad), (0, 0)))
    kb = kp.reshape(B, H, nblk, MOBA_BLOCK, d)
    vb = vp.reshape(B, H, nblk, MOBA_BLOCK, d)
    kmean = jnp.mean(kb.astype(jnp.float32), axis=3)
    n_sel = min(MOBA_TOPK, nblk)
    scale = d ** -0.5
    bias_tab = rel_bias.T.astype(jnp.float32)
    bidx = jnp.arange(B)[:, None, None, None]
    hidx = jnp.arange(H)[None, :, None, None]
    hidx5 = jnp.arange(H)[None, :, None, None, None]
    offs = jnp.arange(MOBA_BLOCK)

    def chunk(ci):
        start = ci * MOBA_Q_CHUNK
        qc = lax.dynamic_slice_in_dim(q, start, MOBA_Q_CHUNK, axis=2)
        qpos = start + jnp.arange(MOBA_Q_CHUNK)
        own = start // MOBA_BLOCK
        gate = jnp.einsum('bhcd,bhnd->bhcn', qc.astype(jnp.float32), kmean)
        gate = jnp.where(jnp.arange(nblk) < own, gate, -jnp.inf)
        gval, sel = lax.top_k(gate, n_sel)
        sel_ok = gval > -jnp.inf
        ks = kb[bidx, hidx, sel]
        vs = vb[bidx, hidx, sel]
        lg_sel = jnp.einsum('bhcd,bhcnkd->bhcnk', qc, ks,
                            preferred_element_type=jnp.float32) * scale
        dist_sel = qpos[None, None, :, None, None] - (sel[..., None] * MOBA_BLOCK + offs)
        lg_sel = lg_sel + bias_tab[hidx5, t5_bucket(dist_sel)]
        lg_sel = jnp.where(sel_ok[..., None], lg_sel, -jnp.inf)
        k_own = lax.dynamic_slice_in_dim(kp, own * MOBA_BLOCK, MOBA_BLOCK, axis=2)
        v_own = lax.dynamic_slice_in_dim(vp, own * MOBA_BLOCK, MOBA_BLOCK, axis=2)
        lg_own = jnp.einsum('bhcd,bhkd->bhck', qc, k_own,
                            preferred_element_type=jnp.float32) * scale
        dist_own = qpos[:, None] - (own * MOBA_BLOCK + offs)[None, :]
        lg_own = lg_own + bias_tab[:, t5_bucket(dist_own)][None]
        lg_own = jnp.where(dist_own >= 0, lg_own, -jnp.inf)
        logits = jnp.concatenate(
            [lg_sel.reshape(B, H, MOBA_Q_CHUNK, n_sel * MOBA_BLOCK), lg_own], axis=-1)
        p = jax.nn.softmax(logits, axis=-1).astype(v.dtype)
        p_sel = p[..., :n_sel * MOBA_BLOCK].reshape(B, H, MOBA_Q_CHUNK, n_sel, MOBA_BLOCK)
        p_own = p[..., n_sel * MOBA_BLOCK:]
        return (jnp.einsum('bhcnk,bhcnkd->bhcd', p_sel, vs)
                + jnp.einsum('bhck,bhkd->bhcd', p_own, v_own))

    out = lax.map(chunk, jnp.arange(S // MOBA_Q_CHUNK))
    return jnp.moveaxis(out, 0, 2).reshape(B, H, S, d)

def hybrid_mixer(x, w_in, b_forget, w_out, rel_bias):
    proj = jnp.einsum('bsd,de->bse', x, w_in)
    cuts = [FOX_W, 2 * FOX_W, 3 * FOX_W, 3 * FOX_W + N_FOX,
            3 * FOX_W + N_FOX + MOBA_W, 3 * FOX_W + N_FOX + 2 * MOBA_W]
    q_f, k_f, v_f, f_logit, q_m, k_m, v_m = jnp.split(proj, cuts, axis=-1)
    log_f = jax.nn.log_sigmoid((f_logit + b_forget).astype(jnp.float32))
    log_f = log_f.transpose(0, 2, 1)
    o_f = fox_attention(split_heads(q_f, N_FOX, HEAD_DIM), split_heads(k_f, N_FOX, HEAD_DIM),
                        split_heads(v_f, N_FOX, HEAD_DIM), log_f)
    o_m = moba_attention(split_heads(q_m, N_MOBA, HEAD_DIM), split_heads(k_m, N_MOBA, HEAD_DIM),
                         split_heads(v_m, N_MOBA, HEAD_DIM), rel_bias)
    o = merge_heads(jnp.concatenate([o_f, o_m.astype(o_f.dtype)], axis=1))
    return jnp.einsum('bse,ed->bsd', o, w_out)

def memory_cross_attention(x, mem, w_q, w_k, w_v, w_o):
    q = split_heads(jnp.einsum('bsd,de->bse', x, w_q), N_CROSS_HEADS, CROSS_HEAD_DIM)
    k = split_heads(jnp.einsum('bmd,de->bme', mem, w_k), N_CROSS_HEADS, CROSS_HEAD_DIM)
    v = split_heads(jnp.einsum('bmd,de->bme', mem, w_v), N_CROSS_HEADS, CROSS_HEAD_DIM)
    logits = jnp.einsum('bhsd,bhmd->bhsm', q, k,
                        preferred_element_type=jnp.float32) * CROSS_HEAD_DIM ** -0.5
    p = jax.nn.softmax(logits, axis=-1).astype(v.dtype)
    o = merge_heads(jnp.einsum('bhsm,bhmd->bhsd', p, v))
    return jnp.einsum('bse,ed->bsd', o, w_o)

def moe_ffn(x, w_router, b_router, w_gate_up, b_gate_up, w_down, b_down):
    B, S, D = x.shape
    T = B * S
    TK = T * TOP_K
    xt = x.reshape(T, D)
    logits = (xt @ w_router + b_router).astype(jnp.float32)
    top_val, top_idx = lax.top_k(logits, TOP_K)
    gates = jax.nn.softmax(top_val, axis=-1)
    e_flat = top_idx.reshape(-1)
    order = jnp.argsort(e_flat)
    e_sorted = e_flat[order]
    counts = jnp.zeros((N_EXPERTS,), jnp.int32).at[e_flat].add(1)
    padded = ((counts + EXPERT_BLOCK - 1) // EXPERT_BLOCK) * EXPERT_BLOCK
    start = jnp.cumsum(counts) - counts
    pend = jnp.cumsum(padded)
    pstart = pend - padded
    rank = jnp.arange(TK, dtype=jnp.int32) - start[e_sorted]
    dest = jnp.zeros((TK,), jnp.int32).at[order].set(pstart[e_sorted] + rank)
    n_blocks = -(-TK // EXPERT_BLOCK) + N_EXPERTS
    n_pad = n_blocks * EXPERT_BLOCK
    slot_token = jnp.full((n_pad,), T, jnp.int32).at[dest].set(
        jnp.arange(TK, dtype=jnp.int32) // TOP_K)
    x_pad = jnp.concatenate([xt, jnp.zeros((1, D), xt.dtype)], axis=0)
    xs = x_pad[slot_token].reshape(n_blocks, EXPERT_BLOCK, D)
    block_expert = jnp.minimum(
        jnp.searchsorted(pend, jnp.arange(n_blocks, dtype=jnp.int32) * EXPERT_BLOCK, side='right'),
        N_EXPERTS - 1)

    def expert_block(args):
        xb, e = args
        h = xb @ w_gate_up[e] + b_gate_up[e]
        g, u = h[:, :D_EXPERT], h[:, D_EXPERT:]
        g = jnp.minimum(g, SWIGLU_LIMIT)
        u = jnp.clip(u, -SWIGLU_LIMIT, SWIGLU_LIMIT)
        glu = g * jax.nn.sigmoid(g * SWIGLU_ALPHA)
        return ((u + 1.0) * glu) @ w_down[e] + b_down[e]

    ys = lax.map(expert_block, (xs, block_expert)).reshape(n_pad, D)
    y = jnp.einsum('tkd,tk->td', ys[dest].reshape(T, TOP_K, D), gates.astype(ys.dtype))
    return y.reshape(B, S, D)

def setup_inputs(seed: int = 0) -> dict:
    key = jax.random.key(seed)
    ks = jax.random.split(key, 24)
    D, L, F, E = D_MODEL, DEPTH, D_EXPERT, N_EXPERTS
    beta = DEEPNORM_BETA

    def nrm(k, shape, scale):
        return jax.random.normal(k, shape, jnp.float32) * scale

    col_scale = jnp.concatenate([
        jnp.ones((2 * FOX_W,), jnp.float32), jnp.full((FOX_W,), beta, jnp.float32),
        jnp.ones((N_FOX + 2 * MOBA_W,), jnp.float32), jnp.full((MOBA_W,), beta, jnp.float32)])
    return {
        "x": nrm(ks[0], (BATCH, SEQ, D), 1.0),
        "mem": nrm(ks[1], (BATCH, N_MEM, D), 1.0),
        "w_in": nrm(ks[2], (L, D, IN_COLS), D ** -0.5) * col_scale,
        "b_forget": 3.0 + nrm(ks[3], (L, N_FOX), 1.0),
        "w_mix_out": nrm(ks[4], (L, D, D), beta * D ** -0.5),
        "rel_bias": nrm(ks[5], (N_BUCKETS, N_MOBA), 0.5),
        "ln1_g": 1.0 + nrm(ks[6], (L, D), 0.02),
        "ln1_b": nrm(ks[7], (L, D), 0.02),
        "w_cq": nrm(ks[8], (L, D, D), D ** -0.5),
        "w_ck": nrm(ks[9], (L, D, D), D ** -0.5),
        "w_cv": nrm(ks[10], (L, D, D), beta * D ** -0.5),
        "w_co": nrm(ks[11], (L, D, D), beta * D ** -0.5),
        "ln2_g": 1.0 + nrm(ks[12], (L, D), 0.02),
        "ln2_b": nrm(ks[13], (L, D), 0.02),
        "w_router": nrm(ks[14], (L, D, E), D ** -0.5),
        "b_router": nrm(ks[15], (L, E), 0.01),
        "w_gate_up": nrm(ks[16], (L, E, D, 2 * F), beta * D ** -0.5),
        "b_gate_up": nrm(ks[17], (L, E, 2 * F), 0.01),
        "w_down": nrm(ks[18], (L, E, F, D), beta * F ** -0.5),
        "b_down": nrm(ks[19], (L, E, D), 0.01),
        "ln3_g": 1.0 + nrm(ks[20], (L, D), 0.02),
        "ln3_b": nrm(ks[21], (L, D), 0.02),
    }

def reference(x, mem, w_in, b_forget, w_mix_out, rel_bias, ln1_g, ln1_b,
              w_cq, w_ck, w_cv, w_co, ln2_g, ln2_b,
              w_router, b_router, w_gate_up, b_gate_up, w_down, b_down,
              ln3_g, ln3_b):
    for l in range(DEPTH):
        h = hybrid_mixer(x, w_in[l], b_forget[l], w_mix_out[l], rel_bias)
        x = layer_norm(DEEPNORM_ALPHA * x + h, ln1_g[l], ln1_b[l])
        h = memory_cross_attention(x, mem, w_cq[l], w_ck[l], w_cv[l], w_co[l])
        x = layer_norm(DEEPNORM_ALPHA * x + h, ln2_g[l], ln2_b[l])
        h = moe_ffn(x, w_router[l], b_router[l], w_gate_up[l], b_gate_up[l],
                    w_down[l], b_down[l])
        x = layer_norm(DEEPNORM_ALPHA * x + h, ln3_g[l], ln3_b[l])
    return x


_drawn_inputs = setup_inputs


def setup_inputs(seed=0):
    import zlib

    import numpy as np

    out = dict(_drawn_inputs(seed))
    spreads = {}
    factors = {'rel_bias': 2.713,
     'b_router': 20.811,
     'b_gate_up': 26.391,
     'b_down': 8.0,
     'ln3_g': 8.725,
     'ln3_b': 8.12}
    for name, (base, spread) in spreads.items():
        noise = np.random.default_rng([zlib.crc32(name.encode()), seed]).standard_normal(out[name].shape)
        drawn = base * np.exp(spread * noise) if base else spread * noise
        out[name] = __import__('jax').numpy.asarray(drawn.astype(out[name].dtype))
    for name, factor in factors.items():
        out[name] = (out[name] * factor).astype(out[name].dtype)
    return out
```

```python
import math
from contextlib import ExitStack

import numpy as np
import concourse.bass as bass
from concourse import mybir

P = 128
D = 1024
T = 256
TT = T // P
KD = D // P
HD = 64
NFOX = 8
NMOBA = 8
NH = NFOX + NMOBA
FW = NFOX * HD
NMEM = 256
NCH = 4
CHD = D // NCH
NE = 32
F = D
TOPK = 4
LIMIT = 7.0
SW_ALPHA = 1.702
ALPHA = 2.0 ** 0.25
EPS = 1e-5
NEG = -1e30
HALF = 512
CAP = 64
NBUCKETS, MAXDIST = 32, 128

XB = T // CAP - 1
NQ = NE * XB
MAXX = (T * TOPK) // CAP
NSTEP = NE + MAXX + 2

C_ID = 0
C_AID = C_ID + P
C_TRI = C_AID + P
C_ONE = C_TRI + P
C_STR = C_ONE + P
C_SEL = C_STR + P
C_MASK = C_SEL + P
C_T5 = C_MASK + 3 * P
C_IO64 = C_T5 + 3 * P
C_IO32 = C_IO64 + CAP
C_EID = C_IO32 + NE
C_BLK = C_EID + 1
C_EPS = C_BLK + 1
NCONST = C_EPS + 1

GROUPS = ["qf", "kf", "vf", "qm", "km", "vm", "ck0", "ck1", "cv0", "cv1",
          "wo0", "wo1", "cq0", "cq1", "co0", "co1"]
GSLOTS = 6
CH = 12
GUC = 8


def t5_bucket(n):
    exact = NBUCKETS // 2
    if n < exact:
        return n
    big = exact + int(np.float32(math.log(n / exact)) / np.float32(math.log(MAXDIST / exact)) * (NBUCKETS - exact))
    return min(big, NBUCKETS - 1)


def constants():
    c = np.zeros((P, NCONST), np.float32)
    i = np.arange(P)
    c[:, C_ID:C_ID + P] = np.eye(P)
    c[:, C_AID:C_AID + P] = np.eye(P) * ALPHA
    c[:, C_TRI:C_TRI + P] = i[:, None] <= i[None, :]
    c[:, C_ONE:C_ONE + P] = 1.0
    c[:, C_STR:C_STR + P] = i[:, None] < i[None, :]
    c[:NQ, C_SEL:C_SEL + P] = (i[:NQ, None] % NE) == i[None, :]
    c[:, C_MASK:C_MASK + P] = np.where(i[None, :] <= i[:, None], 0.0, NEG)
    s = np.arange(2 * P)
    c[:, C_MASK + P:C_MASK + 3 * P] = np.where(s[None, :] <= P + i[:, None], 0.0, NEG)
    for j in range(3 * P):
        n = j - (P - 1)
        if n >= 0:
            c[t5_bucket(n), C_T5 + j] = 1.0
        else:
            c[NBUCKETS, C_T5 + j] = NEG
    c[:, C_IO64:C_IO64 + CAP] = np.arange(1, CAP + 1)
    c[:, C_IO32:C_IO32 + NE] = np.arange(NE)
    c[:, C_EID] = i % NE
    c[:, C_BLK] = CAP * (i // NE + 1)
    c[:, C_EPS] = EPS
    return c


def prefix_jobs():
    order = [("xT", j) for j in range(4)] + [("mT", j) for j in range(4)] + [("t5", 0), ("f", 0)]
    for g in ("qf", "kf", "vf", "qm"):
        order += [(g, 0), (g, 1)]
    order += [("cT", 0)]
    for g in ("km", "vm", "ck0", "ck1", "cv0", "cv1"):
        order += [(g, 0), (g, 1)]
    for s in range(NH + 3):
        if s < NH:
            order += ([("nc", s)] if s < NFOX else []) + [("qk", s)]
        if 0 <= s - 2 < NH:
            order += [("pt", s - 2)]
        if 0 <= s - 3 < NH and (s - 3) % 2 == 0:
            order += [("o", (s - 3) // 2)]
    order += [("wo0", 0), ("wo1", 0), ("wo0", 1), ("wo1", 1)]
    order += [("x1T", j) for j in range(8)]
    for g in ("cq0", "cq1"):
        order += [(g, 0), (g, 1)]
    for s in range(NCH + 2):
        if s < NCH:
            order += [("cqk", s)]
        if 0 <= s - 1 < NCH:
            order += [("cpt", s - 1)]
        if 0 <= s - 2 < NCH:
            order += [("co", s - 2)]
    order += [("co0", 0), ("co1", 0), ("co0", 1), ("co1", 1)]
    order += [("x2T", j) for j in range(8)]
    order += [("router", 0), ("rank", 0), ("tabT", 0), ("tabT", 1), ("pos", 0), ("over", 0)]
    return {name: n for n, name in enumerate(order)}


def hybrid_layer(nc, x, mem, w_in, b_forget, w_mix_out, rel_bias, ln1_g, ln1_b, w_cq, w_ck, w_cv, w_co,
                 ln2_g, ln2_b, w_router, b_router, w_gate_up, b_gate_up, w_down, b_down, ln3_g, ln3_b,
                 consts, out):
    f32, i32, u32 = mybir.dt.float32, mybir.dt.int32, mybir.dt.uint32
    ALU = mybir.AluOpType
    ACT = mybir.ActivationFunctionType
    AX = mybir.AxisListType.X
    JOB = prefix_jobs()
    NJOB = len(JOB)

    ctx = ExitStack()
    with ctx:
        ctx.enter_context(nc.allow_non_contiguous_dma("rows of weights, skewed and broadcast rows"))

        def sb(name, shape, dt=f32):
            return ctx.enter_context(nc.sbuf_tensor(name, shape, dt))

        def sem(name):
            return ctx.enter_context(nc.semaphore(name))

        ring = sb("ring", [P, CH, 2048])
        K = sb("K", [P, NCONST])
        x_nat = sb("x_nat", [P, TT, D])
        reg_a = sb("reg_a", [P, 2048])
        reg_b = sb("reg_b", [P, KD, T])
        reg_c = sb("reg_c", [P, KD, T])
        reg_q = sb("reg_q", [P, 4096])
        reg_k = sb("reg_k", [P, 2048])
        reg_v = sb("reg_v", [P, TT, D])
        kcT = sb("kcT", [P, KD, NMEM])
        vc = sb("vc", [P, 2, D])
        L = sb("L", [P, 4, 512])
        PT = sb("PT", [P, 2, 512])
        NCt = sb("NCt", [P, 2, 3 * P])
        lncol = sb("lncol", [P, 4, KD])
        wf = sb("wf", [P, KD, NFOX])
        bf = sb("bf", [NFOX, 1])
        rel1 = sb("rel1", [NBUCKETS + 1, NMOBA])
        c8 = sb("c8", [P, 3 * P])
        ccol = sb("ccol", [P, TT, NFOX])
        negmax = sb("negmax", [P, NH + NCH, TT])
        psums = sb("psums", [P, NH + NCH, TT])
        rsums = sb("rsums", [P, NH + NCH, TT])
        stats = sb("stats", [P, 3, TT, 2, 6])
        mv = sb("mv", [P, 3, TT, 2])
        rstd = sb("rstd", [P, 3, TT, 2])
        wr = sb("wr", [P, KD, NE])
        brow = sb("brow", [P, NE])
        lg = sb("lg", [P, TT, NE])
        top = sb("top", [P, TT, 8])
        topi = sb("topi", [P, TT, 8], u32)
        topf = sb("topf", [P, TT, 8])
        ntop = sb("ntop", [P, TT])
        M = sb("M", [P, TT, NE])
        E = sb("E", [P, TT, NE])
        gsum = sb("gsum", [P, TT, 2])
        RK = sb("RK", [P, TT, NSTEP])
        GT = sb("GT", [P, TT, NSTEP])
        SEL = sb("SEL", [P, NSTEP])
        cand = sb("cand", [NQ, 4])
        Pq = sb("Pq", [NQ, MAXX])
        ctl = sb("ctl", [1, MAXX + 1], i32)

        lng = reg_q[:, 2048:3072]
        lnb = reg_q[:, 3072:4096]
        t5row = L[0:NMOBA, 0, 0:3 * P]
        after = L[:, :, :].rearrange("p a b -> p (a b)")
        rep = after[:, 0:384].rearrange("p (j t q) -> p j t q", j=2, t=TT)
        repT = after[0:NQ, 384:896].rearrange("p (j t) -> p j t", j=2)
        S = after[:, 896:1152].rearrange("p (t c) -> p t c", t=TT)
        Sg = after[:, 1152:1408].rearrange("p (t c) -> p t c", t=TT)
        SgT = after[:, 1408:1664]
        bsel = after[:, 1664:1792].rearrange("p (i c) -> p i c", i=2)
        fz = PT[0:NFOX, :, :].rearrange("p a b -> p (a b)").rearrange("p (i t) -> p i t", i=4)
        t5t = reg_a[:, :].rearrange("p (h s) -> p h s", h=NMOBA)
        t5rev = t5t[:, :, ::-1]
        mem_nat = reg_a[:, :].rearrange("p (t d) -> p t d", t=2)
        x2 = mem_nat
        qpad = reg_q[:, :].rearrange("p (i e t) -> p i e t", i=NH // 2, e=2)
        kT = reg_k[:, :].rearrange("p (i t) -> p i t", i=NH // 2)
        qcT = reg_q[:, 0:2048].rearrange("p (i t) -> p i t", i=KD)
        xgT = reg_q[:, 0:1024].rearrange("p (k c) -> p k c", k=KD)
        hT = reg_q[:, 1024:1536]
        bgu = kcT[:, :, :].rearrange("p k m -> p (k m)")
        bdn = vc[:, 0, :]
        ysb = vc[:, 1, :]
        Xg = reg_k[:, 0:1024]
        gbuf = reg_k[:, 1024:1536]
        ubuf = reg_k[:, 1536:2048]
        sig = reg_v[:, 0, 0:512]
        gs = reg_v[:, 0, 512:1024]
        hbuf = reg_v[:, 1, 0:512]
        x1 = reg_v
        ident = K[:, C_ID:C_ID + P]

        bank = [ctx.enter_context(nc.psum_tensor(f"bank{b}", [P, HALF], f32)) for b in range(8)]
        gate_ps, up_ps, xy_ps, tr_ps = bank[0], bank[1], bank[2], bank[3]
        acc = [[bank[4], bank[5]], [bank[6], bank[7]]]

        t5_dram = nc.dram_tensor("t5_rows", (NMOBA, 3 * P), f32).ap()

        filled = [sem(f"filled{b}") for b in range(8)]
        evacuated = [sem(f"evacuated{b}") for b in range(8)]
        const_in = sem("const_in")
        x_in = sem("x_in")
        mem_in = sem("mem_in")
        wf_in = sem("wf_in")
        rel_in = sem("rel_in")
        rel_one = sem("rel_one")
        lncol_in = sem("lncol_in")
        ln_in = [sem(f"ln{i}_in") for i in range(3)]
        router_in = sem("router_in")
        bgu_in = sem("bgu_in")
        bdn_in = sem("bdn_in")
        t5_stored = sem("t5_stored")
        t5_in = sem("t5_in")
        group_in = [sem(f"group_in{s}") for s in range(GSLOTS)]
        zeroed = sem("zeroed")
        q_zeroed = sem("q_zeroed")
        dve_step = sem("dve_step")
        act_step = sem("act_step")
        fz_ready = sem("fz_ready")
        fl_ready = sem("fl_ready")
        logits_max = sem("logits_max")
        exp_done = sem("exp_done")
        rsum_ready = sem("rsum_ready")
        probs_ready = sem("probs_ready")
        pv_done = sem("pv_done")
        c8_ready = sem("c8_ready")
        var_ready = sem("var_ready")
        std_ready = sem("std_ready")
        xhat_ready = sem("xhat_ready")
        gained = sem("gained")
        ln_out = sem("ln_out")
        ntop_ready = sem("ntop_ready")
        gexp_ready = sem("gexp_ready")
        mask_ready = sem("mask_ready")
        rep_ready = sem("rep_ready")
        cand_ready = sem("cand_ready")
        pq_ready = sem("pq_ready")
        tables_ready = sem("tables_ready")
        moe_zeroed = sem("moe_zeroed")
        chunk_in = [sem(f"chunk_in{c}") for c in range(CH)]
        chunks_used = sem("chunks_used")
        s_ready = sem("s_ready")
        sg_ready = sem("sg_ready")
        bsel_ready = sem("bsel_ready")
        xg0_done, xg1_done = sem("xg0_done"), sem("xg1_done")
        xg0_sb, xg1_sb = sem("xg0_sb"), sem("xg1_sb")
        xgTa_done, xgTb_done = sem("xgTa_done"), sem("xgTb_done")
        xgTa_sb, xgTb_sb = sem("xgTa_sb"), sem("xgTb_sb")
        gu_done, gu_read = sem("gu_done"), sem("gu_read")
        g_ready, sig_ready, gs_ready, h_ready = sem("g_ready"), sem("sig_ready"), sem("gs_ready"), sem("h_ready")
        hT_done, hT_sb = sem("hT_done"), sem("hT_sb")
        y_done, y_sb = sem("y_done"), sem("y_sb")
        sgT_done, sgT_sb = sem("sgT_done"), sem("sgT_sb")
        scattered = sem("scattered")
        stored = sem("stored")

        def wait_bank(eng, name):
            n = JOB[name]
            if n >= 8:
                eng.wait_ge(evacuated[n % 8], n // 8)

        def wait_filled(eng, name):
            n = JOB[name]
            eng.wait_ge(filled[n % 8], n // 8 + 1)

        def wait_evacuated(eng, name):
            n = JOB[name]
            eng.wait_ge(evacuated[n % 8], n // 8 + 1)

        def B(name):
            return bank[JOB[name] % 8]

        def fill(ins, name):
            ins.then_inc(filled[JOB[name] % 8], 1)

        def evac(ins, name):
            ins.then_inc(evacuated[JOB[name] % 8], 1)

        def group_tile(g):
            s = GROUPS.index(g) % GSLOTS
            return ring[:, 2 * s:2 * s + 2, :].rearrange("p a (b n) -> p (a b) n", n=HALF)

        def wait_group(eng, g):
            n = GROUPS.index(g)
            eng.wait_ge(group_in[n % GSLOTS], 16 * (n // GSLOTS + 1))

        FOX_BASE = {"qf": 0, "kf": FW, "vf": 2 * FW}
        MOBA_BASE = 3 * FW + NFOX
        MOBA = {"qm": MOBA_BASE, "km": MOBA_BASE + FW, "vm": MOBA_BASE + 2 * FW}

        def group_source(g):
            if g in FOX_BASE or g in MOBA:
                c = FOX_BASE[g] if g in FOX_BASE else MOBA[g]
                w = w_in[0][:, c:c + FW]
            else:
                w = {"ck": w_ck, "cv": w_cv, "wo": w_mix_out, "cq": w_cq, "co": w_co}[g[:2]][0]
                w = w[:, int(g[2]) * HALF:(int(g[2]) + 1) * HALF]
            return w.rearrange("(k p) n -> p k n", p=P)

        def chunk_source(e, c):
            if c < GUC:
                w = w_gate_up[0][bass.ds(e, 1), c * P:(c + 1) * P, :]
                return w.rearrange("o p n -> (o p) n")
            w = w_down[0][bass.ds(e, 1), (c - GUC) * 2 * P:(c - GUC + 1) * 2 * P, :]
            return w.rearrange("o (j p) n -> p (o j) n", p=P)

        def chunk_tile(c):
            return ring[:, c, :] if c < GUC else ring[:, c, :].rearrange("p (j n) -> p j n", j=2)

        block = ctx.enter_context(nc.Block())

        @block.sync
        def _(sp):
            for n, g in enumerate(GROUPS):
                if n >= GSLOTS:
                    wait_filled(sp, (GROUPS[n - GSLOTS], 1))
                sp.dma_start(group_tile(g), group_source(g)).then_inc(group_in[n % GSLOTS], 16)

            def load_chunk(e, c):
                sp.dma_start(chunk_tile(c), chunk_source(e, c)).then_inc(chunk_in[c], 16)

            for n in range(len(GROUPS) - GSLOTS, len(GROUPS)):
                wait_filled(sp, (GROUPS[n], 1))
                for c in (2 * (n % GSLOTS), 2 * (n % GSLOTS) + 1):
                    load_chunk(0, c)

            def wait_used(c, n):
                if c == GUC - 1:
                    sp.wait_ge(gu_done, n)
                elif c == CH - 1:
                    sp.wait_ge(y_done, n)
                else:
                    counted = c + 1 if c < GUC else c
                    sp.wait_ge(chunks_used, n * (CH - 2) + (counted - (CH - 2)))

            with sp.Fori(1, NE) as n:
                for c in range(CH):
                    wait_used(c, n)
                    load_chunk(n, c)
            sp.wait_ge(tables_ready, 1)
            pairs = sp.value_load(ctl[0:1, MAXX:MAXX + 1], min_val=0, max_val=MAXX // 2)
            with sp.If(pairs > 0):
                with sp.Fori(0, pairs * 2) as m:
                    e = sp.value_load(ctl[0:1, bass.ds(m, 1)], min_val=0, max_val=NE - 1)
                    for c in range(CH):
                        wait_used(c, m + NE)
                        load_chunk(e, c)
            for tt in range(TT):
                sp.wait_ge(ln_out, 2 * TT + tt + 1)
                sp.dma_start(out[0, tt * P:(tt + 1) * P, :], x_nat[:, tt, :]).then_inc(stored, 16)
            sp.wait_ge(stored, 16 * TT)

        @block.gpsimd
        def _(pool):
            nc.gpsimd.memset(c8[:, :], 0.0)
            nc.gpsimd.memset(RK[:, :, :], 0.0)
            nc.gpsimd.memset(GT[:, :, :], 0.0)
            nc.gpsimd.memset(SEL[:, :], 0.0).then_inc(zeroed, 1)

            def normalise(h, wid):
                pool.wait_ge(rsum_ready, h + 1)
                for tt, (a, b) in enumerate(wid):
                    last = nc.gpsimd.tensor_scalar(L[:, h % 4, a:b], L[:, h % 4, a:b],
                                                   rsums[:, h, tt:tt + 1], None, ALU.mult)
                last.then_inc(probs_ready, 1)

            def ln_bias(i, dst):
                pool.wait_ge(ln_in[i], 32)
                for tt in range(TT):
                    pool.wait_ge(gained, TT * i + tt + 1)
                    nc.gpsimd.tensor_tensor(dst[:, tt, :], dst[:, tt, :], lnb[:, :], ALU.add).then_inc(ln_out, 1)

            for h in range(NH):
                normalise(h, [(0, P), (P, 3 * P)])
            ln_bias(0, x1)
            for h in range(NH, NH + NCH):
                normalise(h, [(0, 256), (256, 512)])
            wait_filled(pool, ("co", NCH - 1))
            nc.gpsimd.memset(bgu, 0.0)
            nc.gpsimd.memset(bdn, 0.0).then_inc(moe_zeroed, 1)
            nc.gpsimd.memset(SgT, 0.0).then_inc(sgT_sb, 1)
            nc.gpsimd.memset(ysb, 0.0).then_inc(y_sb, 1)
            ln_bias(1, x2)

        @block.scalar
        def _(act):
            steps = [0]

            def chain(ins):
                steps[0] += 1
                ins.then_inc(act_step, 1)
                act.wait_ge(act_step, steps[0])

            act.dma_start(x_nat[:, :, :], x[0].rearrange("(t p) d -> p t d", p=P)).then_inc(x_in, 16)
            act.dma_start(K[:, :], consts).then_inc(const_in, 16)
            act.dma_start(mem_nat, mem[0].rearrange("(t p) d -> p t d", p=P)).then_inc(mem_in, 16)
            act.dma_start(wf[:, :, :], w_in[0][:, 3 * FW:3 * FW + NFOX].rearrange("(k p) n -> p k n", p=P)).then_inc(wf_in, 16)
            act.dma_start(bf[:, :], b_forget[0].rearrange("(h o) -> h o", o=1)).then_inc(wf_in, 16)
            act.wait_ge(rel_one, 1)
            act.dma_start(rel1[0:NBUCKETS, :], rel_bias).then_inc(rel_in, 16)
            for i, v in enumerate((ln1_g, ln1_b, ln2_g, ln2_b)):
                act.dma_start(lncol[:, i, :], v[0].rearrange("(k p) -> p k", p=P)).then_inc(lncol_in, 16)
            act.dma_start(wr[:, :, :], w_router[0].rearrange("(k p) n -> p k n", p=P)).then_inc(router_in, 16)
            act.dma_start(brow[:, :], b_router.to_broadcast([P, NE])).then_inc(router_in, 16)

            def load_ln(i, g, b):
                act.dma_start(lng[:, :], g.to_broadcast([P, D])).then_inc(ln_in[i], 16)
                act.dma_start(lnb[:, :], b.to_broadcast([P, D])).then_inc(ln_in[i], 16)


            def copy(name, dst, src=None, scale=1.0):
                wait_filled(act, name)
                evac(nc.scalar.activation(dst, B(name)[:, :] if src is None else src, ACT.Copy, scale=scale), name)

            def copy_q(name, i, scale):
                wait_filled(act, name)
                v = B(name)[:, :].rearrange("p (i t) -> p i t", i=2)
                nc.scalar.activation(qpad[0:64, i:i + 2, 0, :], v[0:64], ACT.Copy, scale=scale)
                evac(nc.scalar.activation(qpad[64:128, i:i + 2, 1, :], v[64:128], ACT.Copy, scale=scale), name)

            for j in (0, 2):
                copy(("xT", j), reg_b[:, 2 * j:2 * j + 2, :], B(("xT", j))[:, :].rearrange("p (a t) -> p a t", a=2))
            for j in (0, 2):
                copy(("mT", j), reg_c[:, 2 * j:2 * j + 2, :], B(("mT", j))[:, :].rearrange("p (a t) -> p a t", a=2))
            copy(("t5", 0), t5row[:, :], B(("t5", 0))[0:NMOBA, 0:3 * P])
            act.wait_ge(evacuated[JOB[("t5", 0)] % 8], JOB[("t5", 0)] // 8 + 1)
            act.dma_start(t5_dram, t5row[:, :]).then_inc(t5_stored, 16)
            act.wait_ge(t5_stored, 16)
            for j in range(4):
                wait_filled(act, ("mT", j))
            act.dma_start(t5t, bass.AP(t5_dram.tensor, t5_dram.offset, [[1, P], [3 * P, NMOBA], [1, 2 * P]])).then_inc(t5_in, 16)
            act.wait_ge(fz_ready, 1)
            chain(nc.scalar.activation(fz[:, 2, :], fz[:, 1, :], ACT.Exp, scale=-1.0))
            nc.scalar.activation(fz[:, 3, :], fz[:, 2, :], ACT.Ln, bias=1.0).then_inc(fl_ready, 1)

            copy_q(("qf", 0), 0, HD ** -0.5)
            copy_q(("qf", 1), 2, HD ** -0.5)
            copy(("vf", 0), reg_v[:, 0, 0:HALF])
            copy_q(("qm", 0), 4, HD ** -0.5)
            copy_q(("qm", 1), 6, HD ** -0.5)
            copy(("vm", 0), reg_v[:, 0, HALF:D])
            for g in range(2):
                for i in range(2):
                    copy((f"cv{g}", i), vc[:, i, g * HALF:(g + 1) * HALF])

            def exps(h, wid, src=None):
                act.wait_ge(logits_max, h + 1)
                for tt, (a, b) in enumerate(wid):
                    s = L[:, h % 4, a:b] if src is None else src[:, a:b]
                    last = nc.scalar.activation(L[:, h % 4, a:b], s, ACT.Exp, bias=negmax[:, h, tt:tt + 1],
                                                accum_out=psums[:, h, tt:tt + 1])
                return last

            for s in range(NH + 3):
                if s < NH:
                    exps(s, [(0, P), (P, 3 * P)]).then_inc(exp_done, 1)
                if 0 <= s - 2 < NH:
                    h = s - 2
                    if h >= 2:
                        if h % 2:
                            wait_filled(act, ("o", (h - 2) // 2))
                        else:
                            act.wait_ge(pv_done, h // 2)
                    copy(("pt", h), PT[:, h % 2, 0:3 * P], B(("pt", h))[:, 0:3 * P])
                if 0 <= s - 3 < NH and (s - 3) % 2 == 1:
                    i = (s - 3) // 2
                    copy(("o", i), reg_c[:, i, :], B(("o", i))[:, 0:T])

            wait_filled(act, ("qk", NH - 1))
            load_ln(0, ln1_g, ln1_b)

            def std(i, tt):
                act.wait_ge(var_ready, TT * i + tt + 1)
                nc.scalar.activation(rstd[:, i, tt, 0:1], mv[:, i, tt, 1:2], ACT.Sqrt,
                                     bias=K[:, C_EPS:C_EPS + 1]).then_inc(std_ready, 1)

            def xT_copies(tag, i):
                for k in range(0, KD, 2):
                    name = (tag, k)
                    wait_filled(act, name)
                    evac(nc.scalar.activation(reg_b[:, k, :], B(name)[:, 0:T], ACT.Identity,
                                              scale=lncol[:, i, k:k + 1], bias=lncol[:, i + 1, k:k + 1]), name)

            for tt in range(TT):
                std(0, tt)
            act.wait_ge(lncol_in, 64)
            xT_copies("x1T", 0)
            copy(("cq0", 0), qcT[:, 0:2, :], B(("cq0", 0))[:, :].rearrange("p (a t) -> p a t", a=2), CHD ** -0.5)
            copy(("cq1", 0), qcT[:, 4:6, :], B(("cq1", 0))[:, :].rearrange("p (a t) -> p a t", a=2), CHD ** -0.5)
            act.wait_ge(ln_out, TT)
            load_ln(1, ln2_g, ln2_b)
            for s in range(NCH + 2):
                if s < NCH:
                    h = NH + s
                    last = exps(h, [(0, 256), (256, 512)], B(("cqk", s)))
                    evac(last, ("cqk", s))
                if 0 <= s - 1 < NCH:
                    h = s - 1
                    if h >= 2:
                        wait_filled(act, ("co", h - 2))
                    copy(("cpt", h), PT[:, h % 2, :])
                if 0 <= s - 2 < NCH:
                    h = s - 2
                    copy(("co", h), reg_c[:, 2 * h:2 * h + 2, :], B(("co", h))[:, :].rearrange("p (a t) -> p a t", a=2))
            act.wait_ge(moe_zeroed, 1)
            act.dma_start(bgu[0:NE, :], b_gate_up[0]).then_inc(bgu_in, 16)
            act.dma_start(bdn[0:NE, :], b_down[0]).then_inc(bdn_in, 16)
            for tt in range(TT):
                std(1, tt)
            xT_copies("x2T", 2)
            act.wait_ge(ln_out, 2 * TT)
            load_ln(2, ln3_g, ln3_b)
            act.wait_ge(ntop_ready, 1)
            for tt in range(TT):
                last = nc.scalar.activation(E[:, tt, :], lg[:, tt, :], ACT.Exp, bias=ntop[:, tt:tt + 1])
            last.then_inc(gexp_ready, 1)

            def evac_xg(half, m):
                act.wait_ge((xg0_done, xg1_done)[half], m)
                nc.scalar.activation(Xg[:, half * HALF:(half + 1) * HALF], (xy_ps, tr_ps)[half][:, :],
                                     ACT.Copy).then_inc((xg0_sb, xg1_sb)[half], 1)

            def evac_xgT(half, m):
                act.wait_ge((xgTa_done, xgTb_done)[half], m)
                nc.scalar.activation(xgT[:, 4 * half:4 * half + 4, :],
                                     (xy_ps, tr_ps)[half][:, :].rearrange("p (k c) -> p k c", k=4),
                                     ACT.Copy).then_inc((xgTa_sb, xgTb_sb)[half], 1)

            for half in range(2):
                evac_xg(half, 1)
            for half in range(2):
                evac_xgT(half, 1)

            def pair(p):
                for i in range(2):
                    act.wait_ge(g_ready, p * 2 + (i + 1))
                    nc.scalar.activation(sig, gbuf, ACT.Sigmoid, scale=SW_ALPHA).then_inc(sig_ready, 1)
                    if i == 0:
                        act.wait_ge(sgT_done, p + 1)
                        act.wait_ge(scattered, p + 1)
                        nc.scalar.activation(SgT[:, :], tr_ps[:, 0:T], ACT.Copy).then_inc(sgT_sb, 1)
                    else:
                        evac_xg(0, p + 2)
                        evac_xg(1, p + 2)
                    act.wait_ge(hT_done, p * 2 + (i + 1))
                    nc.scalar.activation(hT, tr_ps[:, :], ACT.Copy).then_inc(hT_sb, 1)
                    if i == 1:
                        evac_xgT(0, p + 2)
                        evac_xgT(1, p + 2)

            with act.Fori(0, NE // 2) as p:
                pair(p)
            act.wait_ge(tables_ready, 1)
            extra = act.value_load(ctl[0:1, MAXX:MAXX + 1], min_val=0, max_val=MAXX // 2)
            with act.If(extra > 0):
                with act.Fori(NE // 2, extra + NE // 2) as p:
                    pair(p)
            for tt in range(TT):
                std(2, tt)

        @block.vector
        def _(dve):
            steps = [0]

            def chain(ins):
                steps[0] += 1
                ins.then_inc(dve_step, 1)
                dve.wait_ge(dve_step, steps[0])

            def copy(name, dst, src=None):
                wait_filled(dve, name)
                evac(nc.vector.tensor_copy(dst, B(name)[:, :] if src is None else src), name)

            def two(name):
                return B(name)[:, :].rearrange("p (a t) -> p a t", a=2)

            nc.vector.memset(rel1[:, :], 1.0).then_inc(rel_one, 1)
            nc.vector.memset(qpad[64:128, :, 0, :], 0.0)
            nc.vector.memset(qpad[0:64, :, 1, :], 0.0).then_inc(q_zeroed, 1)
            for j in (1, 3):
                copy(("xT", j), reg_b[:, 2 * j:2 * j + 2, :], two(("xT", j)))
            for j in (1, 3):
                copy(("mT", j), reg_c[:, 2 * j:2 * j + 2, :], two(("mT", j)))
            wait_filled(dve, ("f", 0))
            dve.wait_ge(wf_in, 32)
            evac(nc.vector.tensor_scalar(fz[:, 0, :], B(("f", 0))[0:NFOX, 0:T], bf[:, 0:1], None, ALU.add), ("f", 0))
            wait_evacuated(dve, ("f", 0))
            nc.vector.scalar_tensor_tensor(out=fz[:, 1, :], in0=fz[:, 0, :], scalar=-1.0, in1=fz[:, 0, :],
                                           op0=ALU.mult, op1=ALU.max).then_inc(fz_ready, 1)
            dve.wait_ge(fl_ready, 1)
            chain(nc.vector.scalar_tensor_tensor(out=fz[:, 2, :], in0=fz[:, 0, :], scalar=0.0, in1=fz[:, 3, :],
                                                 op0=ALU.min, op1=ALU.subtract))
            dve.wait_ge(const_in, 16)
            dve.wait_ge(zeroed, 1)
            chain(nc.vector.tensor_tensor_scan(c8[0:NFOX, P:3 * P], K[0:NFOX, C_ONE:C_ONE + 1].to_broadcast([NFOX, T]),
                                               fz[:, 2, :], 0.0, ALU.mult, ALU.add))
            nc.vector.tensor_copy(c8[0:NFOX, 0:P], c8[0:NFOX, P:2 * P]).then_inc(c8_ready, 1)

            copy(("kf", 0), kT[:, 0:2, :], two(("kf", 0)))
            copy(("kf", 1), kT[:, 2:4, :], two(("kf", 1)))
            copy(("vf", 1), reg_v[:, 1, 0:HALF])
            name = ("cT", 0)
            copy(name, ccol[:, :, :], B(name)[:, 0:T].rearrange("p (a h) -> p a h", a=TT)[:, :, 0:NFOX])
            copy(("km", 0), kT[:, 4:6, :], two(("km", 0)))
            copy(("km", 1), kT[:, 6:8, :], two(("km", 1)))
            copy(("vm", 1), reg_v[:, 1, HALF:D])
            for g in range(2):
                for i in range(2):
                    name = (f"ck{g}", i)
                    copy(name, kcT[:, 4 * g + 2 * i:4 * g + 2 * i + 2, :], two(name))

            def inverse_sums(h):
                dve.wait_ge(exp_done, h + 1)
                nc.vector.reciprocal(rsums[:, h, :], psums[:, h, :]).then_inc(rsum_ready, 1)

            wait_evacuated(dve, ("cT", 0))
            dve.wait_ge(t5_in, 16)
            for h in range(NH + 1):
                if h < NH:
                    if h < NFOX:
                        name = ("nc", h)
                        wait_filled(dve, name)
                        evac(nc.vector.scalar_tensor_tensor(out=NCt[:, h % 2, :], in0=B(name)[:, 0:3 * P], scalar=-1.0,
                                                            in1=K[:, C_MASK:C_MASK + 3 * P], op0=ALU.mult, op1=ALU.add), name)
                        wait_evacuated(dve, name)
                    name = ("qk", h)
                    wait_filled(dve, name)
                    if h >= 4:
                        wait_filled(dve, ("pt", h - 4))
                    for tt, (a, b) in enumerate([(0, P), (P, 3 * P)]):
                        if h < NFOX:
                            last = nc.vector.scalar_tensor_tensor(out=L[:, h % 4, a:b], in0=B(name)[:, a:b],
                                                                  scalar=ccol[:, tt, h:h + 1], in1=NCt[:, h % 2, a:b],
                                                                  op0=ALU.add, op1=ALU.add)
                        else:
                            last = nc.vector.tensor_tensor(L[:, h % 4, a:b], B(name)[:, a:b],
                                                           t5rev[:, h - NFOX, 2 * P - (b - a):2 * P], ALU.add)
                    evac(last, name)
                    wait_evacuated(dve, name)
                    for tt, (a, b) in enumerate([(0, P), (P, 3 * P)]):
                        last = nc.vector.tensor_reduce(out=negmax[:, h, tt:tt + 1], in_=L[:, h % 4, a:b], op=ALU.max,
                                                       axis=AX, negate=True)
                    last.then_inc(logits_max, 1)
                if h >= 1:
                    inverse_sums(h - 1)

            def residual(i, src, dst, groups):
                for tt in range(TT):
                    for half in range(2):
                        name = (groups[half], tt)
                        wait_filled(dve, name)
                        cols = slice(half * HALF, (half + 1) * HALF)
                        evac(nc.vector.scalar_tensor_tensor(out=dst[:, tt, cols], in0=src[:, tt, cols], scalar=ALPHA,
                                                            in1=B(name)[:, :], op0=ALU.mult, op1=ALU.add), name)
                        wait_evacuated(dve, name)
                        last = nc.vector.bn_stats(stats[:, i, tt, half, :], dst[:, tt, cols])
                    chain(last)
                    nc.vector.bn_aggr(mv[:, i, tt, :], stats[:, i, tt, :, :].rearrange("p a b -> p (a b)")).then_inc(var_ready, 1)
                for tt in range(TT):
                    dve.wait_ge(std_ready, TT * i + tt + 1)
                    chain(nc.vector.reciprocal(rstd[:, i, tt, 1:2], rstd[:, i, tt, 0:1]))
                    nc.vector.tensor_scalar(dst[:, tt, :], dst[:, tt, :], mv[:, i, tt, 0:1], rstd[:, i, tt, 1:2],
                                            ALU.subtract, ALU.mult).then_inc(xhat_ready, 1)

            def xT_copies(tag, i):
                dve.wait_ge(lncol_in, 64)
                for k in range(1, KD, 2):
                    name = (tag, k)
                    wait_filled(dve, name)
                    evac(nc.vector.tensor_scalar(reg_b[:, k, :], B(name)[:, 0:T], lncol[:, i, k:k + 1],
                                                 lncol[:, i + 1, k:k + 1], ALU.mult, ALU.add), name)

            def gain(i, dst, tag):
                dve.wait_ge(ln_in[i], 32)
                for tt in range(TT):
                    nc.vector.tensor_tensor(dst[:, tt, :], dst[:, tt, :], lng[:, :], ALU.mult).then_inc(gained, 1)

            wait_filled(dve, ("o", NH // 2 - 1))
            residual(0, x_nat, x1, ("wo0", "wo1"))
            xT_copies("x1T", 0)
            wait_filled(dve, ("x1T", KD - 1))
            gain(0, x1, "x1T")
            for g in range(2):
                name = (f"cq{g}", 1)
                wait_filled(dve, name)
                evac(nc.vector.tensor_scalar(qcT[:, 4 * g + 2:4 * g + 4, :], two(name), CHD ** -0.5, None, ALU.mult), name)
            for h in range(NCH + 1):
                if h < NCH:
                    name = ("cqk", h)
                    wait_filled(dve, name)
                    if h >= 0:
                        prev = ("pt", NH - 4 + h)
                        wait_filled(dve, prev)
                    nc.vector.tensor_reduce(out=negmax[:, NH + h, :], in_=two(name), op=ALU.max, axis=AX,
                                            negate=True).then_inc(logits_max, 1)
                if h >= 1:
                    dve.wait_ge(evacuated[JOB[("cqk", h - 1)] % 8], JOB[("cqk", h - 1)] // 8 + 1)
                    nc.vector.reciprocal(rsums[:, NH + h - 1, :], psums[:, NH + h - 1, :]).then_inc(rsum_ready, 1)
            dve.wait_ge(ln_out, TT)
            residual(1, x1, x2, ("co0", "co1"))
            xT_copies("x2T", 2)
            wait_filled(dve, ("x2T", KD - 1))
            gain(1, x2, "x2T")

            dve.wait_ge(router_in, 32)
            name = ("router", 0)
            wait_filled(dve, name)
            evac(nc.vector.tensor_tensor(lg[:, :, :], B(name)[:, 0:TT * NE].rearrange("p (a e) -> p a e", a=TT),
                                         brow[:, :].rearrange("p (o e) -> p o e", o=1).to_broadcast([P, TT, NE]), ALU.add), name)
            wait_evacuated(dve, name)
            for tt in range(TT):
                last = nc.vector.max(top[:, tt, :], lg[:, tt, :])
            chain(last)
            nc.vector.tensor_scalar(ntop[:, :], top[:, :, 0], -1.0, None, ALU.mult).then_inc(ntop_ready, 1)
            for tt in range(TT):
                last = nc.vector.max_index(topi[:, tt, :], top[:, tt, :], lg[:, tt, :])
            chain(last)
            chain(nc.vector.tensor_copy(topf[:, :, :], topi[:, :, :]))
            io32 = K[:, C_IO32:C_IO32 + NE]
            for j in range(TOPK):
                for tt in range(TT):
                    if j == 0:
                        last = nc.vector.tensor_scalar(M[:, tt, :], io32, topf[:, tt, 0:1], None, ALU.is_equal)
                    else:
                        last = nc.vector.scalar_tensor_tensor(out=M[:, tt, :], in0=io32, scalar=topf[:, tt, j:j + 1],
                                                              in1=M[:, tt, :], op0=ALU.is_equal, op1=ALU.add)
                if j == TOPK - 1:
                    last.then_inc(mask_ready, 1)
                    dve.wait_ge(mask_ready, 1)
                else:
                    chain(last)
            dve.wait_ge(gexp_ready, 1)
            for tt in range(TT):
                last = nc.vector.scalar_tensor_tensor(out=E[:, tt, :], in0=E[:, tt, :], scalar=1.0, in1=M[:, tt, :],
                                                      op0=ALU.mult, op1=ALU.mult, accum_out=gsum[:, tt, 0:1])
            chain(last)
            chain(nc.vector.reciprocal(gsum[:, :, 1], gsum[:, :, 0]))
            for tt in range(TT):
                nc.vector.tensor_scalar(GT[:, tt, 0:NE], E[:, tt, :], gsum[:, tt, 1:2], None, ALU.mult)
            name = ("rank", 0)
            wait_filled(dve, name)
            chain(nc.vector.tensor_copy(SEL[:, 0:NE], K[:, C_ID:C_ID + NE]))
            evac(nc.vector.tensor_tensor(RK[:, :, 0:NE], B(name)[:, 0:TT * NE].rearrange("p (a e) -> p a e", a=TT),
                                         M[:, :, :], ALU.mult), name)
            wait_evacuated(dve, name)

            for b in range(XB):
                nc.vector.tensor_copy(rep[:, 0, :, b * NE:(b + 1) * NE], RK[:, :, 0:NE])
                last = nc.vector.tensor_copy(rep[:, 1, :, b * NE:(b + 1) * NE], GT[:, :, 0:NE])
            last.then_inc(rep_ready, 1)
            for j in range(2):
                copy(("tabT", j), repT[:, j, :], B(("tabT", j))[0:NQ, 0:T])
            wait_evacuated(dve, ("tabT", 0))
            chain(nc.vector.tensor_reduce(out=cand[:, 0:1], in_=repT[:, 0, :], op=ALU.max, axis=AX))
            chain(nc.vector.tensor_scalar(repT[:, 0, :], repT[:, 0, :], K[0:NQ, C_BLK:C_BLK + 1], None, ALU.subtract))
            nc.vector.tensor_scalar(cand[:, 1:2], cand[:, 0:1], K[0:NQ, C_BLK:C_BLK + 1], None, ALU.is_gt).then_inc(cand_ready, 1)
            dve.wait_ge(cand_ready, 1)
            name = ("pos", 0)
            wait_filled(dve, name)
            evac(nc.vector.tensor_copy(cand[:, 2:3], B(name)[0:NQ, 0:1]), name)
            wait_evacuated(dve, name)
            nc.vector.tensor_scalar(Pq[:, :], K[0:NQ, C_IO32:C_IO32 + MAXX], cand[:, 2:3], cand[:, 1:2],
                                    ALU.is_equal, ALU.mult).then_inc(pq_ready, 1)
            name = ("over", 0)
            wait_filled(dve, name)
            ov = B(name)
            for tt in range(TT):
                nc.vector.tensor_copy(RK[:, tt, NE:NE + MAXX], ov[:, tt * MAXX:(tt + 1) * MAXX])
                nc.vector.tensor_copy(GT[:, tt, NE:NE + MAXX], ov[:, (2 + tt) * MAXX:(3 + tt) * MAXX])
            nc.vector.tensor_copy(SEL[:, NE:NE + MAXX], ov[:, 4 * MAXX:5 * MAXX])
            nc.vector.tensor_copy(ctl[:, 0:MAXX], ov[0:1, 5 * MAXX:6 * MAXX])
            nc.vector.tensor_scalar(ctl[:, MAXX:MAXX + 1], ov[0:1, 6 * MAXX:6 * MAXX + 1], 0.5, 0.25,
                                    ALU.mult, ALU.add).then_inc(tables_ready, 1)
            dve.wait_ge(tables_ready, 1)

            io64 = K[:, C_IO64:C_IO64 + CAP]

            def places(dst, p, gates):
                for i in range(2):
                    for tt in range(TT):
                        rk = RK[:, tt, bass.ds(p * 2 + i, 1)]
                        if gates:
                            last = nc.vector.tensor_scalar(dst[:, tt, i * CAP:(i + 1) * CAP], io64, rk,
                                                           GT[:, tt, bass.ds(p * 2 + i, 1)], ALU.is_equal, ALU.mult)
                        else:
                            last = nc.vector.tensor_scalar(dst[:, tt, i * CAP:(i + 1) * CAP], io64, rk, None, ALU.is_equal)
                return last

            def select(i, step):
                nc.vector.tensor_copy(bsel[:, i, :], SEL[:, bass.ds(step, 1)].to_broadcast([P, CAP])).then_inc(bsel_ready, 1)

            places(S, 0, False).then_inc(s_ready, 1)
            for i in range(2):
                select(i, i)
            places(Sg, 0, True).then_inc(sg_ready, 1)

            def pair(p):
                for i in range(2):
                    n1 = p * 2 + (i + 1)
                    dve.wait_ge(gu_done, n1)
                    nc.vector.tensor_scalar(gbuf, gate_ps[:, :], LIMIT, None, ALU.min).then_inc(g_ready, 1)
                    nc.vector.tensor_scalar(ubuf, up_ps[:, :], LIMIT, -LIMIT, ALU.min, ALU.max).then_inc(gu_read, 1)
                    select(i, p * 2 + (i + 2))
                    dve.wait_ge(sig_ready, n1)
                    dve.wait_ge(g_ready, n1)
                    nc.vector.tensor_tensor(gs, gbuf, sig, ALU.mult).then_inc(gs_ready, 1)
                    dve.wait_ge(gs_ready, n1)
                    dve.wait_ge(gu_read, p * 2 + (i + 2))
                    nc.vector.scalar_tensor_tensor(out=hbuf, in0=ubuf, scalar=1.0, in1=gs,
                                                   op0=ALU.add, op1=ALU.mult).then_inc(h_ready, 1)
                    if i == 0:
                        places(S, p + 1, False).then_inc(s_ready, 1)
                    else:
                        places(Sg, p + 1, True).then_inc(sg_ready, 1)
                    dve.wait_ge(y_done, n1)
                    rows = slice(i * CAP, (i + 1) * CAP)
                    nc.vector.tensor_copy(ysb[rows, 0:HALF], xy_ps[0:CAP, :])
                    nc.vector.tensor_copy(ysb[rows, HALF:D], xy_ps[CAP:P, :]).then_inc(y_sb, 1)

            with dve.Fori(0, NE // 2) as p:
                pair(p)
            extra = dve.value_load(ctl[0:1, MAXX:MAXX + 1], min_val=0, max_val=MAXX // 2)
            with dve.If(extra > 0):
                with dve.Fori(NE // 2, extra + NE // 2) as p:
                    pair(p)

            dve.wait_ge(scattered, extra + (NE // 2 + 1))
            for tt in range(TT):
                for half in range(2):
                    last = nc.vector.bn_stats(stats[:, 2, tt, half, :], acc[tt][half][:, :])
                chain(last)
                nc.vector.bn_aggr(mv[:, 2, tt, :], stats[:, 2, tt, :, :].rearrange("p a b -> p (a b)")).then_inc(var_ready, 1)
            dve.wait_ge(ln_in[2], 32)
            for tt in range(TT):
                dve.wait_ge(std_ready, TT * 2 + tt + 1)
                chain(nc.vector.reciprocal(rstd[:, 2, tt, 1:2], rstd[:, 2, tt, 0:1]))
                for half in range(2):
                    last = nc.vector.tensor_scalar(x_nat[:, tt, half * HALF:(half + 1) * HALF], acc[tt][half][:, :],
                                                   mv[:, 2, tt, 0:1], rstd[:, 2, tt, 1:2], ALU.subtract, ALU.mult)
                chain(last)
                chain(nc.vector.tensor_tensor(x_nat[:, tt, :], x_nat[:, tt, :], lng[:, :], ALU.mult))
                nc.vector.tensor_tensor(x_nat[:, tt, :], x_nat[:, tt, :], lnb[:, :], ALU.add).then_inc(ln_out, 1)

        @block.tensor
        def _(pe):
            mm = nc.tensor.matmul

            pe.wait_ge(const_in, 16)
            for src, tag, arrived in ((x_nat, "xT", x_in), (mem_nat, "mT", mem_in)):
                pe.wait_ge(arrived, 16)
                for j in range(4):
                    name = (tag, j)
                    wait_bank(pe, name)
                    for a in range(2):
                        for tt in range(TT):
                            k = 2 * j + a
                            last = nc.tensor.transpose(B(name)[:, a * T + tt * P:a * T + (tt + 1) * P],
                                                       src[:, tt, k * P:(k + 1) * P], ident)
                    fill(last, name)
            pe.wait_ge(rel_in, 16)
            wait_bank(pe, ("t5", 0))
            fill(mm(B(("t5", 0))[0:NMOBA, 0:3 * P], rel1[:, :], K[0:NBUCKETS + 1, C_T5:C_T5 + 3 * P],
                    start=True, stop=True), ("t5", 0))
            pe.wait_ge(wf_in, 32)
            name = ("f", 0)
            wait_bank(pe, name)
            for j in range(4):
                wait_evacuated(pe, ("xT", j))
            for k in range(KD):
                last = mm(B(name)[0:NFOX, 0:T], wf[:, k, :], reg_b[:, k, :], start=(k == 0), stop=(k == KD - 1))
            fill(last, name)

            def columns_out(g, src):
                w = group_tile(g)
                wait_group(pe, g)
                for j in range(2):
                    name = (g, j)
                    wait_bank(pe, name)
                    for a in range(2):
                        c = (2 * j + a) * P
                        for k in range(KD):
                            last = mm(B(name)[:, a * T:(a + 1) * T], w[:, k, c:c + P], src[:, k, :],
                                      start=(k == 0), stop=(k == KD - 1))
                    fill(last, name)

            def tokens_out(g, src, tt):
                w = group_tile(g)
                wait_group(pe, g)
                name = (g, tt)
                wait_bank(pe, name)
                for k in range(KD):
                    last = mm(B(name)[:, :], src[:, k, tt * P:(tt + 1) * P], w[:, k, :],
                              start=(k == 0), stop=(k == KD - 1))
                fill(last, name)

            columns_out("qf", reg_b)
            columns_out("kf", reg_b)
            for tt in range(TT):
                tokens_out("vf", reg_b, tt)
            columns_out("qm", reg_b)
            name = ("cT", 0)
            pe.wait_ge(c8_ready, 1)
            wait_bank(pe, name)
            for tt in range(TT):
                last = nc.tensor.transpose(B(name)[:, tt * P:(tt + 1) * P], c8[:, P + tt * P:P + (tt + 1) * P], ident)
            fill(last, name)
            columns_out("km", reg_b)
            for tt in range(TT):
                tokens_out("vm", reg_b, tt)
            for j in range(4):
                wait_evacuated(pe, ("mT", j))
            columns_out("ck0", reg_c)
            columns_out("ck1", reg_c)
            for tt in range(TT):
                tokens_out("cv0", reg_c, tt)
            for tt in range(TT):
                tokens_out("cv1", reg_c, tt)

            pe.wait_ge(q_zeroed, 1)
            for g in ("qf", "kf", "qm", "km", "vf", "vm"):
                for j in range(2):
                    wait_evacuated(pe, (g, j))
            for s in range(NH + 3):
                if s < NH:
                    h = s
                    if h < NFOX:
                        name = ("nc", h)
                        wait_bank(pe, name)
                        fill(mm(B(name)[:, 0:3 * P], ident[:, h:h + 1].to_broadcast([P, P]), c8[:, :],
                                start=True, stop=True), name)
                    name = ("qk", h)
                    wait_bank(pe, name)
                    i, e = h // 2, h % 2
                    mm(B(name)[:, 0:P], qpad[:, i, e, 0:P], kT[:, i, 0:P], start=True, stop=True)
                    fill(mm(B(name)[:, P:3 * P], qpad[:, i, e, P:T], kT[:, i, :], start=True, stop=True), name)
                if 0 <= s - 2 < NH:
                    h = s - 2
                    name = ("pt", h)
                    wait_bank(pe, name)
                    pe.wait_ge(probs_ready, h + 1)
                    for a in range(3):
                        last = nc.tensor.transpose(B(name)[:, a * P:(a + 1) * P], L[:, h % 4, a * P:(a + 1) * P], ident)
                    fill(last, name)
                if 0 <= s - 3 < NH:
                    h = s - 3
                    i, e = h // 2, h % 2
                    name = ("o", i)
                    if e == 0:
                        wait_bank(pe, name)
                    wait_evacuated(pe, ("pt", h))
                    rows = slice(e * HD, (e + 1) * HD)
                    cols = slice(h * HD, (h + 1) * HD)
                    mm(B(name)[rows, 0:T], reg_v[:, 0, cols], PT[:, h % 2, 0:T], start=True, stop=False)
                    last = mm(B(name)[rows, P:T], reg_v[:, 1, cols], PT[:, h % 2, T:T + P], start=False, stop=True)
                    if e:
                        fill(last, name)
                    else:
                        last.then_inc(pv_done, 1)

            for i in range(NH // 2):
                wait_evacuated(pe, ("o", i))
            for tt in range(TT):
                for g in ("wo0", "wo1"):
                    tokens_out(g, reg_c, tt)

            def transposes(tag, src, i):
                for tt in range(TT):
                    pe.wait_ge(xhat_ready, TT * i + tt + 1)
                for k in range(KD):
                    name = (tag, k)
                    wait_bank(pe, name)
                    for tt in range(TT):
                        last = nc.tensor.transpose(B(name)[:, tt * P:(tt + 1) * P], src[:, tt, k * P:(k + 1) * P], ident)
                    fill(last, name)
                for k in range(KD):
                    wait_evacuated(pe, (tag, k))

            transposes("x1T", x1, 0)
            columns_out("cq0", reg_b)
            columns_out("cq1", reg_b)

            for g in ("cq0", "cq1", "ck0", "ck1", "cv0", "cv1"):
                for j in range(2):
                    wait_evacuated(pe, (g, j))
            for s in range(NCH + 2):
                if s < NCH:
                    name = ("cqk", s)
                    wait_bank(pe, name)
                    for tt in range(TT):
                        for kk in range(2):
                            last = mm(B(name)[:, tt * NMEM:(tt + 1) * NMEM], qcT[:, 2 * s + kk, tt * P:(tt + 1) * P],
                                      kcT[:, 2 * s + kk, :], start=(kk == 0), stop=(kk == 1))
                    fill(last, name)
                if 0 <= s - 1 < NCH:
                    h = s - 1
                    name = ("cpt", h)
                    wait_bank(pe, name)
                    pe.wait_ge(probs_ready, NH + h + 1)
                    for m in range(2):
                        for tt in range(TT):
                            last = nc.tensor.transpose(B(name)[:, m * T + tt * P:m * T + (tt + 1) * P],
                                                       L[:, h % 4, tt * NMEM + m * P:tt * NMEM + (m + 1) * P], ident)
                    fill(last, name)
                if 0 <= s - 2 < NCH:
                    h = s - 2
                    name = ("co", h)
                    wait_bank(pe, name)
                    wait_evacuated(pe, ("cpt", h))
                    for a in range(2):
                        for m in range(2):
                            last = mm(B(name)[:, a * T:(a + 1) * T], vc[:, m, h * CHD + a * P:h * CHD + (a + 1) * P],
                                      PT[:, h % 2, m * T:(m + 1) * T], start=(m == 0), stop=(m == 1))
                    fill(last, name)
            for h in range(NCH):
                wait_evacuated(pe, ("co", h))
            for tt in range(TT):
                for g in ("co0", "co1"):
                    tokens_out(g, reg_c, tt)
            transposes("x2T", x2, 1)

            pe.wait_ge(router_in, 32)
            name = ("router", 0)
            wait_bank(pe, name)
            for tt in range(TT):
                for k in range(KD):
                    last = mm(B(name)[:, tt * NE:(tt + 1) * NE], reg_b[:, k, tt * P:(tt + 1) * P], wr[:, k, :],
                              start=(k == 0), stop=(k == KD - 1))
            fill(last, name)
            tri, one = K[:, C_TRI:C_TRI + P], K[:, C_ONE:C_ONE + P]
            name = ("rank", 0)
            wait_bank(pe, name)
            pe.wait_ge(mask_ready, 1)
            mm(B(name)[:, 0:NE], tri, M[:, 0, :], start=True, stop=True)
            mm(B(name)[:, NE:2 * NE], one, M[:, 0, :], start=True, stop=False)
            fill(mm(B(name)[:, NE:2 * NE], tri, M[:, 1, :], start=False, stop=True), name)
            pe.wait_ge(rep_ready, 1)
            for j in range(2):
                name = ("tabT", j)
                wait_bank(pe, name)
                for tt in range(TT):
                    last = nc.tensor.transpose(B(name)[0:NQ, tt * P:(tt + 1) * P], rep[:, j, tt, :], ident)
                fill(last, name)
            name = ("pos", 0)
            wait_bank(pe, name)
            pe.wait_ge(cand_ready, 1)
            fill(mm(B(name)[0:NQ, 0:1], K[0:NQ, C_STR:C_STR + NQ], cand[:, 1:2], start=True, stop=True), name)
            name = ("over", 0)
            wait_bank(pe, name)
            pe.wait_ge(pq_ready, 1)
            wait_evacuated(pe, ("tabT", 1))
            ov = B(name)
            for j in range(2):
                for tt in range(TT):
                    c = (2 * j + tt) * MAXX
                    mm(ov[:, c:c + MAXX], repT[:, j, tt * P:(tt + 1) * P], Pq[:, :], start=True, stop=True)
            mm(ov[:, 4 * MAXX:5 * MAXX], K[0:NQ, C_SEL:C_SEL + P], Pq[:, :], start=True, stop=True)
            mm(ov[0:1, 5 * MAXX:6 * MAXX], K[0:NQ, C_EID:C_EID + 1], Pq[:, :], start=True, stop=True)
            fill(mm(ov[0:1, 6 * MAXX:6 * MAXX + 1], K[0:NQ, C_ONE:C_ONE + 1], cand[:, 1:2], start=True, stop=True), name)

            pe.wait_ge(moe_zeroed, 1)
            pe.wait_ge(bgu_in, 16)
            for b in range(8):
                last_job = max(n for n in JOB.values() if n % 8 == b)
                if last_job == JOB[("over", 0)]:
                    pe.wait_ge(tables_ready, 1)
                else:
                    pe.wait_ge(evacuated[b], last_job // 8 + 1)
            pe.sem_inc(gu_read, 1)

            def gather(m):
                pe.wait_ge(s_ready, m)
                for half in range(2):
                    dst = (xy_ps, tr_ps)[half]
                    for tt in range(TT):
                        last = mm(dst[:, :], S[:, tt, :], x2[:, tt, half * HALF:(half + 1) * HALF],
                                  start=(tt == 0), stop=(tt == TT - 1))
                    last.then_inc((xg0_done, xg1_done)[half], 1)

            def transpose_xg(half, m):
                pe.wait_ge((xg0_sb, xg1_sb)[half], m)
                for j in range(4):
                    k = 4 * half + j
                    last = nc.tensor.transpose((xy_ps, tr_ps)[half][:, j * P:(j + 1) * P], Xg[:, k * P:(k + 1) * P], ident)
                last.then_inc((xgTa_done, xgTb_done)[half], 1)

            pe.wait_ge(ln_out, 2 * TT)
            gather(1)
            for tt in range(TT):
                for half in range(2):
                    mm(acc[tt][half][:, :], K[:, C_AID:C_AID + P], x2[:, tt, half * HALF:(half + 1) * HALF],
                       start=True, stop=False, skip_group_check=True)
            for half in range(2):
                transpose_xg(half, 1)
            pe.wait_ge(bdn_in, 16)
            for tt in range(TT):
                for half in range(2):
                    mm(acc[tt][half][:, :], repT[:, 1, tt * P:(tt + 1) * P], bdn[0:NQ, half * HALF:(half + 1) * HALF],
                       start=False, stop=False, skip_group_check=True)

            def scatter():
                for tt in range(TT):
                    for half in range(2):
                        last = mm(acc[tt][half][:, :], SgT[:, tt * P:(tt + 1) * P], ysb[:, half * HALF:(half + 1) * HALF],
                                  start=False, stop=False, skip_group_check=True)
                last.then_inc(scattered, 1)

            def gate_up(p, i):
                n = p * 2 + i
                pe.wait_ge(gu_read, n + 1)
                pe.wait_ge(bsel_ready, n + 1)
                for ps, c0 in ((gate_ps, 0), (up_ps, F)):
                    for half in range(2):
                        c = c0 + half * HALF
                        mm(ps[half * CAP:(half + 1) * CAP, :], bsel[:, i, :], bgu[:, c:c + HALF], start=True, stop=False)
                if i == 0:
                    pe.wait_ge(xgTa_sb, p + 1)
                for k in range(KD):
                    if i == 0 and k == KD // 2:
                        pe.wait_ge(xgTb_sb, p + 1)
                    pe.wait_ge(chunk_in[k], n * 16 + 16)
                    for ps, c0 in ((gate_ps, 0), (up_ps, F)):
                        for half in range(2):
                            c = c0 + half * HALF
                            last = mm(ps[half * CAP:(half + 1) * CAP, :], xgT[:, k, i * CAP:(i + 1) * CAP],
                                      ring[:, k, c:c + HALF], start=False, stop=(k == KD - 1))
                    if k < KD - 1:
                        last.then_inc(chunks_used, 1)
                last.then_inc(gu_done, 1)

            def transpose_h(n1):
                pe.wait_ge(h_ready, n1)
                for j in range(4):
                    last = nc.tensor.transpose(tr_ps[:, j * P:(j + 1) * P], hbuf[:, j * P:(j + 1) * P], ident)
                last.then_inc(hT_done, 1)

            def down(p, n, ks):
                for k in ks:
                    c, j = GUC + k // 2, k % 2
                    if j == 0:
                        pe.wait_ge(chunk_in[c], n * 16 + 16)
                    w = chunk_tile(c)
                    a = (k % 4) * P + (k // 4) * CAP
                    for half in range(2):
                        last = mm(xy_ps[half * CAP:(half + 1) * CAP, :], hT[:, a:a + CAP],
                                  w[:, j, half * HALF:(half + 1) * HALF], start=(k == 0), stop=(k == KD - 1))
                    if j and k < KD - 1:
                        last.then_inc(chunks_used, 1)
                if k == KD - 1:
                    last.then_inc(y_done, 1)

            def pair(p):
                gate_up(p, 0)
                pe.wait_ge(y_sb, p * 2 + 1)
                pe.wait_ge(sgT_sb, p + 1)
                scatter()
                pe.wait_ge(sg_ready, p + 1)
                pe.wait_ge(xgTb_sb, p + 1)
                for tt in range(TT):
                    last = nc.tensor.transpose(tr_ps[:, tt * P:(tt + 1) * P], Sg[:, tt, :], ident)
                last.then_inc(sgT_done, 1)
                pe.wait_ge(sgT_sb, p + 2)
                transpose_h(p * 2 + 1)
                pe.wait_ge(hT_sb, p * 2 + 1)
                down(p, p * 2, range(KD))
                gate_up(p, 1)
                pe.wait_ge(y_sb, p * 2 + 2)
                gather(p + 2)
                pe.wait_ge(xg1_sb, p + 2)
                transpose_h(p * 2 + 2)
                transpose_xg(0, p + 2)
                pe.wait_ge(hT_sb, p * 2 + 2)
                pe.wait_ge(xgTa_sb, p + 2)
                down(p, p * 2 + 1, range(KD // 2))
                transpose_xg(1, p + 2)
                down(p, p * 2 + 1, range(KD // 2, KD))

            with pe.Fori(0, NE // 2) as p:
                pair(p)
            pe.wait_ge(tables_ready, 1)
            extra = pe.value_load(ctl[0:1, MAXX:MAXX + 1], min_val=0, max_val=MAXX // 2)
            with pe.If(extra > 0):
                with pe.Fori(NE // 2, extra + NE // 2) as p:
                    pair(p)
            pe.wait_ge(y_sb, extra * 2 + (NE + 1))
            pe.wait_ge(sgT_sb, extra + (NE // 2 + 1))
            scatter()


INS = ["x", "mem", "w_in", "b_forget", "w_mix_out", "rel_bias", "ln1_g", "ln1_b", "w_cq", "w_ck", "w_cv", "w_co",
       "ln2_g", "ln2_b", "w_router", "b_router", "w_gate_up", "b_gate_up", "w_down", "b_down", "ln3_g", "ln3_b"]


def kernel(**inputs):
    import concourse.bacc as bacc
    from concourse.bass_utils import run_bass_kernel_spmd

    nc = bacc.Bacc("TRN2", target_bir_lowering=False, num_devices=1)
    arrays = {f"in_{n}": np.ascontiguousarray(inputs[n]) for n in INS}
    arrays["in_consts"] = constants()
    args = [nc.dram_tensor(n, a.shape, mybir.dt.from_np(a.dtype), kind="ExternalInput").ap() for n, a in arrays.items()]
    out = nc.dram_tensor("out", (1, T, D), mybir.dt.float32, kind="ExternalOutput").ap()
    hybrid_layer(nc, *args, out)
    r = run_bass_kernel_spmd(nc, [arrays], core_ids=[0])
    return r.results[0]["out"]
```

```python
import math
from contextlib import ExitStack

import numpy as np
import concourse.bass as bass
from concourse import mybir

P = 128
D = 1024
T = 256
TT = T // P
KD = D // P
HD = 64
NFOX = 8
NMOBA = 8
NH = NFOX + NMOBA
FW = NFOX * HD
NMEM = 256
NCH = 4
CHD = D // NCH
NE = 32
F = D
TOPK = 4
LIMIT = 7.0
SW_ALPHA = 1.702
ALPHA = 2.0 ** 0.25
EPS = 1e-5
NEG = -1e30
HALF = 512
CAP = 64
NBUCKETS, MAXDIST = 32, 128

XB = T // CAP - 1
NQ = NE * XB
MAXX = (T * TOPK) // CAP
NSTEP = NE + MAXX + 2

C_ID = 0
C_AID = C_ID + P
C_TRI = C_AID + P
C_ONE = C_TRI + P
C_STR = C_ONE + P
C_SEL = C_STR + P
C_MASK = C_SEL + P
C_T5 = C_MASK + 3 * P
C_IO64 = C_T5 + 3 * P
C_IO32 = C_IO64 + CAP
C_EID = C_IO32 + NE
C_BLK = C_EID + 1
C_EPS = C_BLK + 1
C_STK = C_EPS + 1
NCONST = C_STK + NE

GROUPS = ["qf", "kf", "vf", "qm", "km", "vm", "ck0", "ck1", "cv0", "wo0",
          "wo1", "cv1", "cq0", "cq1", "co0", "co1"]
GSLOTS = 6
CH = 12
GUC = 8


def t5_bucket(n):
    exact = NBUCKETS // 2
    if n < exact:
        return n
    big = exact + int(np.float32(math.log(n / exact)) / np.float32(math.log(MAXDIST / exact)) * (NBUCKETS - exact))
    return min(big, NBUCKETS - 1)


def constants():
    c = np.zeros((P, NCONST), np.float32)
    i = np.arange(P)
    c[:, C_ID:C_ID + P] = np.eye(P)
    c[:, C_AID:C_AID + P] = np.eye(P) * ALPHA
    c[:, C_TRI:C_TRI + P] = i[:, None] <= i[None, :]
    c[:, C_ONE:C_ONE + P] = 1.0
    c[:, C_STR:C_STR + P] = i[:, None] < i[None, :]
    c[:NQ, C_SEL:C_SEL + P] = (i[:NQ, None] % NE) == i[None, :]
    c[:, C_MASK:C_MASK + P] = np.where(i[None, :] <= i[:, None], 0.0, NEG)
    s = np.arange(2 * P)
    c[:, C_MASK + P:C_MASK + 3 * P] = np.where(s[None, :] <= P + i[:, None], 0.0, NEG)
    for j in range(3 * P):
        n = j - (P - 1)
        if n >= 0:
            c[t5_bucket(n), C_T5 + j] = 1.0
        else:
            c[NBUCKETS, C_T5 + j] = NEG
    c[:, C_IO64:C_IO64 + CAP] = np.arange(1, CAP + 1)
    c[:, C_IO32:C_IO32 + NE] = np.arange(NE)
    c[:, C_EID] = i % NE
    c[:, C_BLK] = CAP * (i // NE + 1)
    c[:, C_EPS] = EPS
    c[:, C_STK:C_STK + NE] = (i[:, None] % NE) == np.arange(NE)[None, :]
    return c


MIXER = [("p", "qm", 0), ("a", 0), ("p", "qm", 1), ("a", 1), ("p", "km", 0), ("a", 2), ("p", "km", 1), ("a", 3),
         ("p", "vm", 0), ("p", "vm", 1), ("a", 4), ("a", 5), ("p", "ck0", 0), ("a", 6), ("a", 7), ("p", "ck0", 1),
         ("a", 8), ("a", 9), ("p", "ck1", 0), ("a", 10), ("a", 11), ("a", 12), ("p", "ck1", 1), ("a", 13), ("a", 14),
         ("p", "cv0", 0), ("a", 15), ("a", 16), ("p", "cv0", 1), ("a", 17), ("a", 18),
         ("p", "wo0", 0), ("p", "wo1", 0), ("p", "wo0", 1), ("p", "wo1", 1), ("p", "cv1", 0)]
CROSS = [("p", "cq0", 0), ("p", "cq0", 1), ("a", 0), ("p", "cq1", 0), ("a", 1), ("p", "cq1", 1), ("a", 2),
         ("a", 3), ("p", "cv1", 1), ("a", 4), ("a", 5)]


def prefix_jobs():
    order = [("xT", j) for j in range(4)] + [("f", 0)]
    order += [("qf", 0), ("qf", 1), ("t5", 0)]
    order += [("kf", 0), ("kf", 1)] + [("mT", j) for j in range(4)]
    order += [("vf", 0), ("vf", 1), ("cT", 0)]
    for what, *n in MIXER:
        if what == "p":
            order += [tuple(n)]
            continue
        s = n[0]
        if s < NH:
            order += ([("nc", s)] if s < NFOX else []) + [("qk", s)]
        if 0 <= s - 2 < NH:
            order += [("pt", s - 2)]
        if 0 <= s - 3 < NH and (s - 3) % 2 == 0:
            order += [("o", (s - 3) // 2)]
    order += [("x1T", tt, h) for tt in range(TT) for h in range(2)]
    for what, *n in CROSS:
        if what == "p":
            order += [tuple(n)]
            continue
        s = n[0]
        order += ([("cqk", s)] if s < NCH else []) + ([("cpt", s - 1)] if 0 <= s - 1 < NCH else [])
        order += [("co", s - 2)] if 0 <= s - 2 < NCH else []
    order += [("co0", 0), ("co1", 0), ("co0", 1), ("co1", 1)]
    order += [("x2T", tt, h) for tt in range(TT) for h in range(2)]
    order += [("rpart", 0), ("router", 0), ("rank", 0)]
    return {name: n for n, name in enumerate(order)}


def hybrid_layer(nc, x, mem, w_in, b_forget, w_mix_out, rel_bias, ln1_g, ln1_b, w_cq, w_ck, w_cv, w_co,
                 ln2_g, ln2_b, w_router, b_router, w_gate_up, b_gate_up, w_down, b_down, ln3_g, ln3_b,
                 consts, out):
    f32, i32, u32 = mybir.dt.float32, mybir.dt.int32, mybir.dt.uint32
    ALU = mybir.AluOpType
    ACT = mybir.ActivationFunctionType
    AX = mybir.AxisListType.X
    JOB = prefix_jobs()
    NJOB = len(JOB)

    ctx = ExitStack()
    with ctx:
        ctx.enter_context(nc.allow_non_contiguous_dma("rows of weights, skewed and broadcast rows"))

        def sb(name, shape, dt=f32):
            return ctx.enter_context(nc.sbuf_tensor(name, shape, dt))

        def sem(name):
            return ctx.enter_context(nc.semaphore(name))

        ring = sb("ring", [P, CH, 2048])
        K = sb("K", [P, NCONST])
        x_nat = sb("x_nat", [P, TT, D])
        reg_a = sb("reg_a", [P, 2048])
        reg_b = sb("reg_b", [P, KD, T])
        reg_c = sb("reg_c", [P, KD, T])
        reg_q = sb("reg_q", [P, 4096])
        reg_k = sb("reg_k", [P, 2048])
        reg_v = sb("reg_v", [P, TT, D])
        kcT = sb("kcT", [P, KD, NMEM])
        vc = sb("vc", [P, 2, D])
        L = sb("L", [P, 4, 512])
        PT = sb("PT", [P, 2, 512])
        NCt = sb("NCt", [P, 2, 3 * P])
        lncol = sb("lncol", [P, 4, KD])
        wf = sb("wf", [P, KD, NFOX])
        bf = sb("bf", [NFOX, 1])
        rel1 = sb("rel1", [NBUCKETS + 1, NMOBA])
        c8 = sb("c8", [P, 3 * P])
        ccol = sb("ccol", [P, TT, NFOX])
        negmax = sb("negmax", [P, NH + NCH, TT])
        psums = sb("psums", [P, NH + NCH, TT])
        rsums = sb("rsums", [P, NH + NCH, TT])
        stats = sb("stats", [P, 3, TT, 2, 6])
        mv = sb("mv", [P, 3, TT, 2])
        rstd = sb("rstd", [P, 3, TT, 2])
        wr = sb("wr", [P, KD, NE])
        brow = sb("brow", [P, NE])
        lg = sb("lg", [P, TT, NE])
        top = sb("top", [P, TT, 8])
        topi = sb("topi", [P, TT, 8], u32)
        topf = sb("topf", [P, TT, 8])
        ntop = sb("ntop", [P, TT])
        warm = sb("warm", [P, 5])
        M = sb("M", [P, TT, NE])
        eq4 = NCt[:, 1, 0:TT * TOPK * NE].rearrange("p (t j e) -> p t j e", t=TT, j=TOPK)
        E = sb("E", [P, TT, NE])
        gsum = sb("gsum", [P, TT, 2])
        RK = sb("RK", [P, TT, NSTEP])
        GT = sb("GT", [P, TT, NSTEP])
        SEL = sb("SEL", [P, NSTEP])
        cand = sb("cand", [NQ, 4])
        Pq = sb("Pq", [NQ, MAXX])
        ctl = sb("ctl", [1, MAXX + 1], i32)

        lng = reg_q[:, 2048:3072]
        lnb = reg_q[:, 3072:4096]
        t5row = L[0:NMOBA, 0, 0:3 * P]
        after = L[:, :, :].rearrange("p a b -> p (a b)")
        rep = after[:, 0:384].rearrange("p (j t q) -> p j t q", j=2, t=TT)
        repT = after[0:NQ, 384:896].rearrange("p (j t) -> p j t", j=2)
        S = after[:, 896:1152].rearrange("p (t c) -> p t c", t=TT)
        Sg = after[:, 1152:1408].rearrange("p (t c) -> p t c", t=TT)
        SgT = after[:, 1408:1664]
        bsel = after[:, 1664:1792].rearrange("p (i c) -> p i c", i=2)
        fz = PT[0:NFOX, :, :].rearrange("p a b -> p (a b)").rearrange("p (i t) -> p i t", i=4)
        t5t = reg_a[:, :].rearrange("p (h s) -> p h s", h=NMOBA)
        t5rev = t5t[:, :, ::-1]
        mem_nat = reg_a[:, :].rearrange("p (t d) -> p t d", t=2)
        x2 = mem_nat
        qpad = reg_q[:, :].rearrange("p (i e t) -> p i e t", i=NH // 2, e=2)
        kT = reg_k[:, :].rearrange("p (i t) -> p i t", i=NH // 2)
        qcT = reg_q[:, 0:2048].rearrange("p (i t) -> p i t", i=KD)
        xgT = PT[:, :, :].rearrange("p a b -> p (a b)").rearrange("p (k c) -> p k c", k=KD)
        hT = NCt[:, :, :].rearrange("p a b -> p (a b)")[:, 0:512]
        bgu = kcT[:, :, :].rearrange("p k m -> p (k m)")
        bdn = vc[:, 0, :]
        memT = reg_c
        ocT = reg_k[:, :].rearrange("p (k t) -> p k t", k=KD)
        oT = reg_b
        ysb = vc[:, 1, :]
        Xg = reg_k[:, 0:1024]
        gbuf = reg_k[:, 1024:1536]
        ubuf = reg_k[:, 1536:2048]
        sig = reg_v[:, 0, 0:512]
        gs = reg_v[:, 0, 512:1024]
        hbuf = reg_v[:, 1, 0:512]
        x1 = reg_v
        ident = K[:, C_ID:C_ID + P]

        bank = [ctx.enter_context(nc.psum_tensor(f"bank{b}", [P, HALF], f32)) for b in range(8)]
        gate_ps, up_ps, xy_ps, tr_ps = bank[0], bank[1], bank[2], bank[3]
        acc = [[bank[4], bank[5]], [bank[6], bank[7]]]

        t5_dram = nc.dram_tensor("t5_rows", (NMOBA, 3 * P), f32).ap()

        filled = [sem(f"filled{b}") for b in range(8)]
        evacuated = [sem(f"evacuated{b}") for b in range(8)]
        ident_in = sem("ident_in")
        const_in = sem("const_in")
        x_in = sem("x_in")
        mem_in = sem("mem_in")
        wf_in = sem("wf_in")
        rel_in = sem("rel_in")
        rel_one = sem("rel_one")
        lncol_in = sem("lncol_in")
        ln_in = [sem(f"ln{i}_in") for i in range(3)]
        router_in = sem("router_in")
        bgu_in = sem("bgu_in")
        bdn_in = sem("bdn_in")
        t5_stored = sem("t5_stored")
        t5_in = sem("t5_in")
        group_in = [sem(f"group_in{s}") for s in range(GSLOTS)]
        zeroed = sem("zeroed")
        q_zeroed = sem("q_zeroed")
        dve_step = sem("dve_step")
        act_step = sem("act_step")
        fz_ready = sem("fz_ready")
        fl_ready = sem("fl_ready")
        logits_max = sem("logits_max")
        exp_done = sem("exp_done")
        rsum_ready = sem("rsum_ready")
        probs_ready = sem("probs_ready")
        pv_done = sem("pv_done")
        c8_ready = sem("c8_ready")
        var_ready = sem("var_ready")
        std_ready = sem("std_ready")
        xhat_ready = sem("xhat_ready")
        gained = sem("gained")
        ln_out = sem("ln_out")
        ntop_ready = sem("ntop_ready")
        gexp_ready = sem("gexp_ready")
        mask_ready = sem("mask_ready")
        rep_ready = sem("rep_ready")
        cand_ready = sem("cand_ready")
        pq_ready = sem("pq_ready")
        tab_done, tab_sb, pos_done, over_done = sem("tab_done"), sem("tab_sb"), sem("pos_done"), sem("over_done")
        tables_ready = sem("tables_ready")
        moe_zeroed = sem("moe_zeroed")
        chunk_in = [sem(f"chunk_in{c}") for c in range(CH)]
        chunks_used = sem("chunks_used")
        s_ready = sem("s_ready")
        sg_ready = sem("sg_ready")
        bsel_ready = sem("bsel_ready")
        xg0_done, xg1_done = sem("xg0_done"), sem("xg1_done")
        xg0_sb, xg1_sb = sem("xg0_sb"), sem("xg1_sb")
        xgTa_done, xgTb_done = sem("xgTa_done"), sem("xgTb_done")
        xgTa_sb, xgTb_sb = sem("xgTa_sb"), sem("xgTb_sb")
        gu_done, gu_read = sem("gu_done"), sem("gu_read")
        g_ready, sig_ready, gs_ready, h_ready = sem("g_ready"), sem("sig_ready"), sem("gs_ready"), sem("h_ready")
        hT_done, hT_sb = sem("hT_done"), sem("hT_sb")
        y_done, y_sb = sem("y_done"), sem("y_sb")
        sgT_done, sgT_sb = sem("sgT_done"), sem("sgT_sb")
        scattered = sem("scattered")
        tile_done = sem("tile_done")
        scale_ready = sem("scale_ready")
        normed = sem("normed")
        gained3 = sem("gained3")
        biased_pool, biased_dve = sem("biased_pool"), sem("biased_dve")
        stored = sem("stored")

        def wait_bank(eng, name):
            n = JOB[name]
            if n >= 8:
                eng.wait_ge(evacuated[n % 8], n // 8)

        def wait_filled(eng, name):
            n = JOB[name]
            eng.wait_ge(filled[n % 8], n // 8 + 1)

        def wait_evacuated(eng, name):
            n = JOB[name]
            eng.wait_ge(evacuated[n % 8], n // 8 + 1)

        def B(name):
            return bank[JOB[name] % 8]

        def fill(ins, name):
            ins.then_inc(filled[JOB[name] % 8], 1)

        def evac(ins, name):
            ins.then_inc(evacuated[JOB[name] % 8], 1)

        def group_tile(g):
            s = GROUPS.index(g) % GSLOTS
            return ring[:, 2 * s:2 * s + 2, :].rearrange("p a (b n) -> p (a b) n", n=HALF)

        def wait_group(eng, g):
            n = GROUPS.index(g)
            eng.wait_ge(group_in[n % GSLOTS], 16 * (n // GSLOTS + 1))

        FOX_BASE = {"qf": 0, "kf": FW, "vf": 2 * FW}
        MOBA_BASE = 3 * FW + NFOX
        MOBA = {"qm": MOBA_BASE, "km": MOBA_BASE + FW, "vm": MOBA_BASE + 2 * FW}

        def group_source(g):
            if g in FOX_BASE or g in MOBA:
                c = FOX_BASE[g] if g in FOX_BASE else MOBA[g]
                w = w_in[0][:, c:c + FW]
            else:
                w = {"ck": w_ck, "cv": w_cv, "wo": w_mix_out, "cq": w_cq, "co": w_co}[g[:2]][0]
                w = w[:, int(g[2]) * HALF:(int(g[2]) + 1) * HALF]
            return w.rearrange("(k p) n -> p k n", p=P)

        def chunk_source(e, c):
            if c < GUC:
                w = w_gate_up[0][bass.ds(e, 1), c * P:(c + 1) * P, :]
                return w.rearrange("o p n -> (o p) n")
            w = w_down[0][bass.ds(e, 1), (c - GUC) * 2 * P:(c - GUC + 1) * 2 * P, :]
            return w.rearrange("o (j p) n -> p (o j) n", p=P)

        def in_slot(s, c):
            return ring[:, s, :] if c < GUC else ring[:, s, :].rearrange("p (j n) -> p j n", j=2)

        early = [x_nat[:, :, :].rearrange("p t d -> p (t d)"), reg_q[:, 0:2048], reg_c[:, :, :].rearrange("p k t -> p (k t)"),
                 reg_q[:, 2048:4096], reg_b[:, :, :].rearrange("p k t -> p (k t)")]

        NEARLY = len(early)

        def chunk_tile(c, e=None):
            if e == 0:
                return in_slot(c, c)
            if e == 1 and c < NEARLY:
                return early[c]
            return in_slot((c - NEARLY) % CH, c)

        block = ctx.enter_context(nc.Block())

        @block.sync
        def _(sp):
            def load_small(g):
                if g == "qf":
                    sp.dma_start(K[:, 0:P], consts[:, 0:P]).then_inc(ident_in, 16)
                    for tt in range(TT):
                        sp.dma_start(x_nat[:, tt, :], x[0, tt * P:(tt + 1) * P, :]).then_inc(x_in, 16)
                    sp.dma_start(wf[:, :, :], w_in[0][:, 3 * FW:3 * FW + NFOX].rearrange("(k p) n -> p k n", p=P)).then_inc(wf_in, 16)
                    sp.dma_start(bf[:, :], b_forget[0].rearrange("(h o) -> h o", o=1)).then_inc(wf_in, 16)
                elif g == "kf":
                    sp.dma_start(K[:, P:NCONST], consts[:, P:NCONST]).then_inc(const_in, 16)
                    sp.wait_ge(rel_one, 1)
                    sp.dma_start(rel1[0:NBUCKETS, :], rel_bias).then_inc(rel_in, 16)
                elif g == "vf":
                    sp.dma_start(mem_nat, mem[0].rearrange("(t p) d -> p t d", p=P)).then_inc(mem_in, 16)
                elif g == "vm":
                    for i, v in enumerate((ln1_g, ln1_b, ln2_g, ln2_b)):
                        sp.dma_start(lncol[:, i, :], v[0].rearrange("(k p) -> p k", p=P)).then_inc(lncol_in, 16)
                    sp.dma_start(wr[:, :, :], w_router[0].rearrange("(k p) n -> p k n", p=P)).then_inc(router_in, 16)
                    sp.dma_start(brow[:, :], b_router.to_broadcast([P, NE])).then_inc(router_in, 16)

            for n, g in enumerate(GROUPS):
                load_small(g)
                if n >= GSLOTS:
                    wait_filled(sp, (GROUPS[n - GSLOTS], 1))
                sp.dma_start(group_tile(g), group_source(g)).then_inc(group_in[n % GSLOTS], 16)

            def load_chunk(e, c, fixed=None):
                sp.dma_start(chunk_tile(c, fixed), chunk_source(e, c)).then_inc(chunk_in[c], 16)

            def load_early(c, left):
                if c == 0:
                    wait_evacuated(sp, left)
                elif left:
                    wait_filled(sp, left)
                sp.wait_ge(chunk_in[c], 16)
                sp.dma_start(early[c], chunk_source(1, c)).then_inc(chunk_in[c], 16)

            def wait_used(c, n):
                if c == GUC - 1:
                    sp.wait_ge(gu_done, n)
                elif c == CH - 1:
                    sp.wait_ge(y_done, n)
                else:
                    counted = c + 1 if c < GUC else c
                    sp.wait_ge(chunks_used, n * (CH - 2) + (counted - (CH - 2)))

            for n in sorted(range(len(GROUPS) - GSLOTS, len(GROUPS)), key=lambda n: JOB[GROUPS[n], 1]):
                if GROUPS[n] == "co0":
                    load_early(0, ("wo1", 1))
                    load_early(2, ("cv1", 1))
                    load_early(1, ("cqk", NCH - 1))
                wait_filled(sp, (GROUPS[n], 1))
                for c in (2 * (n % GSLOTS), 2 * (n % GSLOTS) + 1):
                    load_chunk(0, c, 0)
            sp.wait_ge(ln_out, 2 * TT)
            load_early(3, None)
            load_early(4, ("rpart", 0))
            for c in range(NEARLY, CH):
                wait_used(c - NEARLY, 1)
                sp.wait_ge(chunk_in[c], 16)
                load_chunk(1, c)
            for c in range(CH):
                if c < NEARLY:
                    wait_used(c - NEARLY + CH, 1)
                    sp.wait_ge(chunk_in[c], 32)
                else:
                    wait_used(c, 2)
                load_chunk(2, c)
            with sp.Fori(3, NE) as n:
                for c in range(CH):
                    wait_used(c, n)
                    load_chunk(n, c)
            sp.wait_ge(tables_ready, 1)
            pairs = sp.value_load(ctl[0:1, MAXX:MAXX + 1], min_val=0, max_val=MAXX // 2)
            with sp.If(pairs > 0):
                with sp.Fori(0, pairs * 2) as m:
                    e = sp.value_load(ctl[0:1, bass.ds(m, 1)], min_val=0, max_val=NE - 1)
                    for c in range(CH):
                        wait_used(c, m + NE)
                        load_chunk(e, c)
            for tt in range(TT):
                for half in range(2):
                    cols = slice(half * HALF, (half + 1) * HALF)
                    sp.wait_ge((biased_pool, biased_dve)[half], tt + 1)
                    sp.dma_start(out[0, tt * P:(tt + 1) * P, cols], x_nat[:, tt, cols]).then_inc(stored, 16)
            sp.wait_ge(stored, 16 * TT * 2)

        @block.gpsimd
        def _(pool):
            nc.gpsimd.memset(c8[:, :], 0.0)
            nc.gpsimd.memset(RK[:, :, :], 0.0)
            nc.gpsimd.memset(GT[:, :, :], 0.0)
            nc.gpsimd.memset(SEL[:, :], 0.0).then_inc(zeroed, 1)

            def normalise(h, wid):
                pool.wait_ge(rsum_ready, h + 1)
                for tt, (a, b) in enumerate(wid):
                    last = nc.gpsimd.tensor_scalar(L[:, h % 4, a:b], L[:, h % 4, a:b],
                                                   rsums[:, h, tt:tt + 1], None, ALU.mult)
                last.then_inc(probs_ready, 1)

            def gain_and_bias(i, dst, tag):
                pool.wait_ge(ln_in[i], 32)
                for tt in range(TT):
                    wait_filled(pool, (tag, tt, 1))
                    nc.gpsimd.tensor_tensor(dst[:, tt, :], dst[:, tt, :], lng, ALU.mult).then_inc(gained, 1)
                    pool.wait_ge(gained, TT * i + tt + 1)
                    nc.gpsimd.tensor_tensor(dst[:, tt, :], dst[:, tt, :], lnb, ALU.add).then_inc(ln_out, 1)

            for h in range(NH):
                normalise(h, [(0, P), (P, 3 * P)])
            gain_and_bias(0, x1, "x1T")
            for h in range(NH, NH + NCH):
                normalise(h, [(0, 256), (256, 512)])
            wait_filled(pool, ("co", NCH - 1))
            nc.gpsimd.memset(bgu, 0.0)
            nc.gpsimd.memset(bdn, 0.0).then_inc(moe_zeroed, 1)
            gain_and_bias(1, x2, "x2T")
            pool.wait_ge(ln_in[2], 32)
            for tt in range(TT):
                pool.wait_ge(gained3, 2 * tt + 1)
                nc.gpsimd.tensor_tensor(x_nat[:, tt, 0:HALF], x_nat[:, tt, 0:HALF], lnb[:, 0:HALF],
                                        ALU.add).then_inc(biased_pool, 1)

        @block.scalar
        def _(act):
            steps = [0]

            def chain(ins):
                steps[0] += 1
                ins.then_inc(act_step, 1)
                act.wait_ge(act_step, steps[0])

            def load_ln(i, g, b):
                act.dma_start(lng[:, :], g.to_broadcast([P, D])).then_inc(ln_in[i], 16)
                act.dma_start(lnb[:, :], b.to_broadcast([P, D])).then_inc(ln_in[i], 16)


            def copy(name, dst, src=None, scale=1.0):
                wait_filled(act, name)
                evac(nc.scalar.activation(dst, B(name)[:, :] if src is None else src, ACT.Copy, scale=scale), name)

            def copy_q(name, i, scale):
                wait_filled(act, name)
                v = B(name)[:, :].rearrange("p (i t) -> p i t", i=2)
                nc.scalar.activation(qpad[0:64, i:i + 2, 0, :], v[0:64], ACT.Copy, scale=scale)
                evac(nc.scalar.activation(qpad[64:128, i:i + 2, 1, :], v[64:128], ACT.Copy, scale=scale), name)

            for j in (0, 2):
                copy(("xT", j), reg_b[:, 2 * j:2 * j + 2, :], B(("xT", j))[:, :].rearrange("p (a t) -> p a t", a=2))
            act.wait_ge(fz_ready, 1)
            chain(nc.scalar.activation(fz[:, 2, :], fz[:, 1, :], ACT.Exp, scale=-1.0))
            nc.scalar.activation(fz[:, 3, :], fz[:, 2, :], ACT.Ln, bias=1.0).then_inc(fl_ready, 1)
            copy_q(("qf", 0), 0, HD ** -0.5)
            copy_q(("qf", 1), 2, HD ** -0.5)
            copy(("t5", 0), t5row, B(("t5", 0))[0:NMOBA, 0:3 * P])
            wait_evacuated(act, ("t5", 0))
            act.dma_start(t5_dram, t5row).then_inc(t5_stored, 16)
            for j in (0, 2):
                copy(("mT", j), reg_c[:, 2 * j:2 * j + 2, :], B(("mT", j))[:, :].rearrange("p (a t) -> p a t", a=2))
            act.wait_ge(t5_stored, 16)
            wait_filled(act, ("mT", 3))
            act.dma_start(t5t, bass.AP(t5_dram.tensor, t5_dram.offset, [[1, P], [3 * P, NMOBA], [1, 2 * P]])).then_inc(t5_in, 16)
            copy(("vf", 0), reg_v[:, 0, 0:HALF])

            def evac_projection(g, j):
                if g == "qm":
                    copy_q((g, j), 4 + 2 * j, HD ** -0.5)
                elif (g, j) == ("vm", 0):
                    copy((g, j), reg_v[:, 0, HALF:D])
                elif g[:2] == "cv":
                    c = int(g[2]) * HALF
                    copy((g, j), vc[:, j, c:c + HALF])
                elif g[:2] == "cq" and j == 0:
                    i = 4 * int(g[2])
                    copy((g, j), qcT[:, i:i + 2, :], B((g, j))[:, :].rearrange("p (a t) -> p a t", a=2), CHD ** -0.5)

            def exps(h, wid, src=None):
                act.wait_ge(logits_max, h + 1)
                for tt, (a, b) in enumerate(wid):
                    s = L[:, h % 4, a:b] if src is None else src[:, a:b]
                    last = nc.scalar.activation(L[:, h % 4, a:b], s, ACT.Exp, bias=negmax[:, h, tt:tt + 1],
                                                accum_out=psums[:, h, tt:tt + 1])
                return last

            for what, *n in MIXER:
                if what == "p":
                    if n[0] == "cv1":
                        nc.scalar.activation(warm[:, 0:1], K[:, C_EPS:C_EPS + 1], ACT.Sqrt)
                        continue
                    evac_projection(*n)
                    continue
                s = n[0]
                if s < NH:
                    exps(s, [(0, P), (P, 3 * P)]).then_inc(exp_done, 1)
                if 0 <= s - 2 < NH:
                    h = s - 2
                    if h >= 2:
                        if h % 2:
                            wait_filled(act, ("o", (h - 2) // 2))
                        else:
                            act.wait_ge(pv_done, h // 2)
                    copy(("pt", h), PT[:, h % 2, 0:3 * P], B(("pt", h))[:, 0:3 * P])
                if 0 <= s - 3 < NH and (s - 3) % 2 == 1:
                    i = (s - 3) // 2
                    copy(("o", i), oT[:, i, :], B(("o", i))[:, 0:T])

            wait_filled(act, ("qk", NH - 1))
            load_ln(0, ln1_g, ln1_b)

            def std(i, tt):
                act.wait_ge(var_ready, TT * i + tt + 1)
                nc.scalar.activation(rstd[:, i, tt, 0:1], mv[:, i, tt, 1:2], ACT.Sqrt,
                                     bias=K[:, C_EPS:C_EPS + 1]).then_inc(std_ready, 1)

            def xT_copy(tag, i, tt):
                name = (tag, tt, 0)
                wait_filled(act, name)
                for k in range(4):
                    last = nc.scalar.activation(reg_b[:, k, tt * P:(tt + 1) * P], B(name)[:, k * P:(k + 1) * P],
                                                ACT.Identity, scale=lncol[:, i, k:k + 1], bias=lncol[:, i + 1, k:k + 1])
                evac(last, name)

            act.wait_ge(lncol_in, 64)
            act.wait_ge(const_in, 16)
            std(0, 0)
            std(0, 1)
            evac_projection("cv1", 0)
            xT_copy("x1T", 0, 0)
            xT_copy("x1T", 0, 1)
            for what, *n in CROSS:
                if what == "p":
                    evac_projection(*n)
                    continue
                s = n[0]
                if s < NCH:
                    evac(exps(NH + s, [(0, 256), (256, 512)], B(("cqk", s))), ("cqk", s))
                if 0 <= s - 1 < NCH:
                    h = s - 1
                    if h >= 2:
                        wait_filled(act, ("co", h - 2))
                    copy(("cpt", h), PT[:, h % 2, :])
                if 0 <= s - 2 < NCH:
                    h = s - 2
                    copy(("co", h), ocT[:, 2 * h:2 * h + 2, :], B(("co", h))[:, :].rearrange("p (a t) -> p a t", a=2))
            act.wait_ge(ln_out, TT)
            load_ln(1, ln2_g, ln2_b)
            nc.scalar.activation(warm[:, 1:2], K[:, C_EPS:C_EPS + 1], ACT.Sqrt)
            act.wait_ge(moe_zeroed, 1)
            act.dma_start(bgu[0:NE, :], b_gate_up[0]).then_inc(bgu_in, 16)
            act.dma_start(bdn[0:NE, :], b_down[0]).then_inc(bdn_in, 16)
            for tt in range(TT):
                std(1, tt)
                xT_copy("x2T", 2, tt)
            nc.scalar.activation(warm[:, 2:3], K[:, C_EPS:C_EPS + 1], ACT.Exp)
            act.wait_ge(ntop_ready, 1)
            for tt in range(TT):
                last = nc.scalar.activation(E[:, tt, :], lg[:, tt, :], ACT.Exp, bias=ntop[:, tt:tt + 1])
            last.then_inc(gexp_ready, 1)
            nc.scalar.activation(warm[:, 3:4], K[:, C_EPS:C_EPS + 1], ACT.Sigmoid)

            def evac_xg(half, m):
                act.wait_ge((xg0_done, xg1_done)[half], m)
                nc.scalar.activation(Xg[:, half * HALF:(half + 1) * HALF], (xy_ps, tr_ps)[half][:, :],
                                     ACT.Copy).then_inc((xg0_sb, xg1_sb)[half], 1)

            def evac_xgT(half, m):
                act.wait_ge((xgTa_done, xgTb_done)[half], m)
                nc.scalar.activation(xgT[:, 4 * half:4 * half + 4, :],
                                     (xy_ps, tr_ps)[half][:, :].rearrange("p (k c) -> p k c", k=4),
                                     ACT.Copy).then_inc((xgTa_sb, xgTb_sb)[half], 1)

            for half in range(2):
                evac_xg(half, 1)
            for half in range(2):
                evac_xgT(half, 1)

            def pair(p, first=False):
                for i in range(2):
                    act.wait_ge(g_ready, p * 2 + (i + 1))
                    nc.scalar.activation(sig, gbuf, ACT.Sigmoid, scale=SW_ALPHA).then_inc(sig_ready, 1)
                    if i == 0:
                        act.wait_ge(sgT_done, p + 1)
                        if not first:
                            act.wait_ge(scattered, p)
                        nc.scalar.activation(SgT[:, :], tr_ps[:, 0:T], ACT.Copy).then_inc(sgT_sb, 1)
                    else:
                        evac_xg(0, p + 2)
                        evac_xg(1, p + 2)
                    act.wait_ge(hT_done, p * 2 + (i + 1))
                    nc.scalar.activation(hT, tr_ps[:, :], ACT.Copy).then_inc(hT_sb, 1)
                    if i == 1:
                        evac_xgT(0, p + 2)
                        evac_xgT(1, p + 2)

            pair(0, first=True)
            load_ln(2, ln3_g, ln3_b)
            with act.Fori(1, NE // 2) as p:
                pair(p)
            act.wait_ge(tables_ready, 1)
            extra = act.value_load(ctl[0:1, MAXX:MAXX + 1], min_val=0, max_val=MAXX // 2)
            with act.If(extra > 0):
                with act.Fori(NE // 2, extra + NE // 2) as p:
                    pair(p)
            nc.scalar.activation(warm[:, 4:5], K[:, C_EPS:C_EPS + 1], ACT.Sqrt)
            for tt in range(TT):
                std(2, tt)
            for tt in range(TT):
                act.wait_ge(scale_ready, tt + 1)
                for half in range(2):
                    nc.scalar.activation(x_nat[:, tt, half * HALF:(half + 1) * HALF], acc[tt][half][:, :], ACT.Identity,
                                         scale=rstd[:, 2, tt, 1:2], bias=mv[:, 2, tt, 1:2]).then_inc(normed, 1)

        @block.vector
        def _(dve):
            steps = [0]

            def chain(ins):
                steps[0] += 1
                ins.then_inc(dve_step, 1)
                dve.wait_ge(dve_step, steps[0])

            def copy(name, dst, src=None):
                wait_filled(dve, name)
                evac(nc.vector.tensor_copy(dst, B(name)[:, :] if src is None else src), name)

            def two(name):
                return B(name)[:, :].rearrange("p (a t) -> p a t", a=2)

            nc.vector.memset(rel1[:, :], 1.0).then_inc(rel_one, 1)
            nc.vector.memset(qpad[64:128, :, 0, :], 0.0)
            nc.vector.memset(qpad[0:64, :, 1, :], 0.0).then_inc(q_zeroed, 1)
            for j in (1, 3):
                copy(("xT", j), reg_b[:, 2 * j:2 * j + 2, :], two(("xT", j)))
            wait_filled(dve, ("f", 0))
            dve.wait_ge(wf_in, 32)
            evac(nc.vector.tensor_scalar(fz[:, 0, :], B(("f", 0))[0:NFOX, 0:T], bf[:, 0:1], None, ALU.add), ("f", 0))
            wait_evacuated(dve, ("f", 0))
            nc.vector.scalar_tensor_tensor(out=fz[:, 1, :], in0=fz[:, 0, :], scalar=-1.0, in1=fz[:, 0, :],
                                           op0=ALU.mult, op1=ALU.max).then_inc(fz_ready, 1)
            dve.wait_ge(fl_ready, 1)
            chain(nc.vector.scalar_tensor_tensor(out=fz[:, 2, :], in0=fz[:, 0, :], scalar=0.0, in1=fz[:, 3, :],
                                                 op0=ALU.min, op1=ALU.subtract))
            dve.wait_ge(const_in, 16)
            dve.wait_ge(zeroed, 1)
            chain(nc.vector.tensor_tensor_scan(c8[0:NFOX, P:3 * P], K[0:NFOX, C_ONE:C_ONE + 1].to_broadcast([NFOX, T]),
                                               fz[:, 2, :], 0.0, ALU.mult, ALU.add))
            nc.vector.tensor_copy(c8[0:NFOX, 0:P], c8[0:NFOX, P:2 * P]).then_inc(c8_ready, 1)

            copy(("kf", 0), kT[:, 0:2, :], two(("kf", 0)))
            copy(("kf", 1), kT[:, 2:4, :], two(("kf", 1)))
            for j in (1, 3):
                copy(("mT", j), reg_c[:, 2 * j:2 * j + 2, :], two(("mT", j)))
            copy(("vf", 1), reg_v[:, 1, 0:HALF])
            name = ("cT", 0)
            copy(name, ccol[:, :, :], B(name)[:, 0:T].rearrange("p (a h) -> p a h", a=TT)[:, :, 0:NFOX])

            def evac_projection(g, j):
                if g == "km":
                    copy((g, j), kT[:, 4 + 2 * j:6 + 2 * j, :], two((g, j)))
                elif (g, j) == ("vm", 1):
                    copy((g, j), reg_v[:, 1, HALF:D])
                elif g[:2] == "ck":
                    i = 4 * int(g[2]) + 2 * j
                    copy((g, j), kcT[:, i:i + 2, :], two((g, j)))
                elif g[:2] == "cq" and j == 1:
                    i = 4 * int(g[2]) + 2
                    wait_filled(dve, (g, j))
                    evac(nc.vector.tensor_scalar(qcT[:, i:i + 2, :], two((g, j)), CHD ** -0.5, None, ALU.mult), (g, j))

            def inverse_sums(h):
                dve.wait_ge(exp_done, h + 1)
                nc.vector.reciprocal(rsums[:, h, :], psums[:, h, :]).then_inc(rsum_ready, 1)

            wait_evacuated(dve, ("cT", 0))
            dve.wait_ge(t5_in, 16)
            for what, *item in MIXER:
                if what == "p":
                    evac_projection(*item)
                    continue
                h = item[0]
                if 1 <= h <= NH:
                    inverse_sums(h - 1)
                if h < NH:
                    if h < NFOX:
                        name = ("nc", h)
                        wait_filled(dve, name)
                        evac(nc.vector.scalar_tensor_tensor(out=NCt[:, h % 2, :], in0=B(name)[:, 0:3 * P], scalar=-1.0,
                                                            in1=K[:, C_MASK:C_MASK + 3 * P], op0=ALU.mult, op1=ALU.add), name)
                        wait_evacuated(dve, name)
                    name = ("qk", h)
                    wait_filled(dve, name)
                    if h >= 4:
                        wait_filled(dve, ("pt", h - 4))
                    for tt, (a, b) in enumerate([(0, P), (P, 3 * P)]):
                        if h < NFOX:
                            last = nc.vector.scalar_tensor_tensor(out=L[:, h % 4, a:b], in0=B(name)[:, a:b],
                                                                  scalar=ccol[:, tt, h:h + 1], in1=NCt[:, h % 2, a:b],
                                                                  op0=ALU.add, op1=ALU.add)
                        else:
                            last = nc.vector.tensor_tensor(L[:, h % 4, a:b], B(name)[:, a:b],
                                                           t5rev[:, h - NFOX, 2 * P - (b - a):2 * P], ALU.add)
                    evac(last, name)
                    wait_evacuated(dve, name)
                    for tt, (a, b) in enumerate([(0, P), (P, 3 * P)]):
                        last = nc.vector.tensor_reduce(out=negmax[:, h, tt:tt + 1], in_=L[:, h % 4, a:b], op=ALU.max,
                                                       axis=AX, negate=True)
                    last.then_inc(logits_max, 1)

            def residual(i, src, dst, groups, tag):
                for tt in range(TT):
                    for half in range(2):
                        name = (groups[half], tt)
                        wait_filled(dve, name)
                        cols = slice(half * HALF, (half + 1) * HALF)
                        evac(nc.vector.scalar_tensor_tensor(out=dst[:, tt, cols], in0=src[:, tt, cols], scalar=ALPHA,
                                                            in1=B(name)[:, :], op0=ALU.mult, op1=ALU.add), name)
                        wait_evacuated(dve, name)
                        last = nc.vector.bn_stats(stats[:, i, tt, half, :], dst[:, tt, cols])
                    chain(last)
                    nc.vector.bn_aggr(mv[:, i, tt, :], stats[:, i, tt, :, :].rearrange("p a b -> p (a b)")).then_inc(var_ready, 1)
                    dve.wait_ge(var_ready, TT * i + tt + 1)
                    dve.wait_ge(std_ready, TT * i + tt + 1)
                    chain(nc.vector.reciprocal(rstd[:, i, tt, 1:2], rstd[:, i, tt, 0:1]))
                    for half in range(2):
                        cols = slice(half * HALF, (half + 1) * HALF)
                        nc.vector.tensor_scalar(dst[:, tt, cols], dst[:, tt, cols], mv[:, i, tt, 0:1], rstd[:, i, tt, 1:2],
                                                ALU.subtract, ALU.mult).then_inc(xhat_ready, 1)
                dve.wait_ge(lncol_in, 64)
                for tt in range(TT):
                    name = (tag, tt, 1)
                    wait_filled(dve, name)
                    for k in range(4):
                        last = nc.vector.tensor_scalar(reg_b[:, 4 + k, tt * P:(tt + 1) * P], B(name)[:, k * P:(k + 1) * P],
                                                       lncol[:, 2 * i, 4 + k:5 + k], lncol[:, 2 * i + 1, 4 + k:5 + k],
                                                       ALU.mult, ALU.add)
                    evac(last, name)

            wait_filled(dve, ("o", NH // 2 - 1))
            residual(0, x_nat, x1, ("wo0", "wo1"), "x1T")
            for what, *item in CROSS:
                if what == "p":
                    evac_projection(*item)
                    continue
                h = item[0]
                if 1 <= h <= NCH:
                    wait_evacuated(dve, ("cqk", h - 1))
                    nc.vector.reciprocal(rsums[:, NH + h - 1, :], psums[:, NH + h - 1, :]).then_inc(rsum_ready, 1)
                if h < NCH:
                    name = ("cqk", h)
                    wait_filled(dve, name)
                    nc.vector.tensor_reduce(out=negmax[:, NH + h, :], in_=two(name), op=ALU.max, axis=AX,
                                            negate=True).then_inc(logits_max, 1)
            dve.wait_ge(ln_out, TT)
            residual(1, x1, x2, ("co0", "co1"), "x2T")

            dve.wait_ge(zeroed, 1)
            nc.vector.tensor_copy(SEL[:, 0:NE], K[:, C_ID:C_ID + NE])
            copy(("rpart", 0), NCt[:, 0, 0:T], B(("rpart", 0))[:, 0:T])
            dve.wait_ge(router_in, 32)
            name = ("router", 0)
            wait_filled(dve, name)
            evac(nc.vector.tensor_tensor(lg[:, :, :], B(name)[:, 0:TT * NE].rearrange("p (a e) -> p a e", a=TT),
                                         brow[:, :].rearrange("p (o e) -> p o e", o=1).to_broadcast([P, TT, NE]), ALU.add), name)
            wait_evacuated(dve, name)
            for tt in range(TT):
                last = nc.vector.max(top[:, tt, :], lg[:, tt, :])
            chain(last)
            nc.vector.tensor_scalar(ntop[:, :], top[:, :, 0], -1.0, None, ALU.mult).then_inc(ntop_ready, 1)
            for tt in range(TT):
                last = nc.vector.max_index(topi[:, tt, :], top[:, tt, :], lg[:, tt, :])
            chain(last)
            chain(nc.vector.tensor_copy(topf[:, :, :], topi[:, :, :]))
            io32 = K[:, C_IO32:C_IO32 + NE]
            chain(nc.vector.tensor_tensor(eq4[:, :, :, :], io32.rearrange("p (t j e) -> p t j e", t=1, j=1).to_broadcast([P, TT, TOPK, NE]),
                                          topf[:, :, 0:TOPK].rearrange("p t (j e) -> p t j e", e=1).to_broadcast([P, TT, TOPK, NE]),
                                          ALU.is_equal))
            nc.vector.tensor_reduce(out=M[:, :, :], in_=eq4[:, :, :, :].rearrange("p t j e -> p t e j"), op=ALU.add,
                                    axis=AX).then_inc(mask_ready, 1)
            dve.wait_ge(mask_ready, 1)
            name = ("rank", 0)
            wait_filled(dve, name)
            evac(nc.vector.tensor_tensor(RK[:, :, 0:NE], B(name)[:, 0:TT * NE].rearrange("p (a e) -> p a e", a=TT),
                                         M[:, :, :], ALU.mult), name)
            wait_evacuated(dve, name)
            io64 = K[:, C_IO64:C_IO64 + CAP]

            def places(dst, p, gates):
                for i in range(2):
                    for tt in range(TT):
                        rk = RK[:, tt, bass.ds(p * 2 + i, 1)]
                        if gates:
                            last = nc.vector.tensor_scalar(dst[:, tt, i * CAP:(i + 1) * CAP], io64, rk,
                                                           GT[:, tt, bass.ds(p * 2 + i, 1)], ALU.is_equal, ALU.mult)
                        else:
                            last = nc.vector.tensor_scalar(dst[:, tt, i * CAP:(i + 1) * CAP], io64, rk, None, ALU.is_equal)
                return last

            places(S, 0, False).then_inc(s_ready, 1)
            dve.wait_ge(gexp_ready, 1)
            for tt in range(TT):
                last = nc.vector.scalar_tensor_tensor(out=E[:, tt, :], in0=E[:, tt, :], scalar=1.0, in1=M[:, tt, :],
                                                      op0=ALU.mult, op1=ALU.mult, accum_out=gsum[:, tt, 0:1])
            chain(last)
            chain(nc.vector.reciprocal(gsum[:, :, 1], gsum[:, :, 0]))
            for tt in range(TT):
                last = nc.vector.tensor_scalar(GT[:, tt, 0:NE], E[:, tt, :], gsum[:, tt, 1:2], None, ALU.mult)
            chain(last)

            def further_blocks():
                dve.wait_ge(tab_done, 1)
                nc.vector.tensor_copy(repT[:, :, :], xy_ps[0:NQ, :].rearrange("p (j t) -> p j t", j=2)).then_inc(tab_sb, 1)
                dve.wait_ge(tab_sb, 1)
                chain(nc.vector.tensor_reduce(out=cand[:, 0:1], in_=repT[:, 0, :], op=ALU.max, axis=AX))
                chain(nc.vector.tensor_scalar(repT[:, 0, :], repT[:, 0, :], K[0:NQ, C_BLK:C_BLK + 1], None, ALU.subtract))
                nc.vector.tensor_scalar(cand[:, 1:2], cand[:, 0:1], K[0:NQ, C_BLK:C_BLK + 1], None, ALU.is_gt).then_inc(cand_ready, 1)
                dve.wait_ge(cand_ready, 1)
                dve.wait_ge(pos_done, 1)
                chain(nc.vector.tensor_copy(cand[:, 2:3], xy_ps[0:NQ, 0:1]))
                nc.vector.tensor_scalar(Pq[:, :], K[0:NQ, C_IO32:C_IO32 + MAXX], cand[:, 2:3], cand[:, 1:2],
                                        ALU.is_equal, ALU.mult).then_inc(pq_ready, 1)
                dve.wait_ge(over_done, 1)
                ov = xy_ps
                for tt in range(TT):
                    nc.vector.tensor_copy(RK[:, tt, NE:NE + MAXX], ov[:, tt * MAXX:(tt + 1) * MAXX])
                    nc.vector.tensor_copy(GT[:, tt, NE:NE + MAXX], ov[:, (2 + tt) * MAXX:(3 + tt) * MAXX])
                nc.vector.tensor_copy(SEL[:, NE:NE + MAXX], ov[:, 4 * MAXX:5 * MAXX])
                nc.vector.tensor_copy(ctl[:, 0:MAXX], ov[0:1, 5 * MAXX:6 * MAXX])
                nc.vector.tensor_scalar(ctl[:, MAXX:MAXX + 1], ov[0:1, 6 * MAXX:6 * MAXX + 1], 0.5, 0.25,
                                        ALU.mult, ALU.add).then_inc(tables_ready, 1)
                dve.wait_ge(tables_ready, 1)

            def select(i, step):
                nc.vector.tensor_copy(bsel[:, i, :], SEL[:, bass.ds(step, 1)].to_broadcast([P, CAP])).then_inc(bsel_ready, 1)

            for i in range(2):
                select(i, i)
            places(Sg, 0, True).then_inc(sg_ready, 1)
            for b in range(XB):
                nc.vector.tensor_copy(rep[:, 0, :, b * NE:(b + 1) * NE], RK[:, :, 0:NE])
                last = nc.vector.tensor_copy(rep[:, 1, :, b * NE:(b + 1) * NE], GT[:, :, 0:NE])
            last.then_inc(rep_ready, 1)

            def pair(p, first=False):
                for i in range(2):
                    n1 = p * 2 + (i + 1)
                    dve.wait_ge(gu_done, n1)
                    nc.vector.tensor_scalar(gbuf, gate_ps[:, :], LIMIT, None, ALU.min).then_inc(g_ready, 1)
                    nc.vector.tensor_scalar(ubuf, up_ps[:, :], LIMIT, -LIMIT, ALU.min, ALU.max).then_inc(gu_read, 1)
                    select(i, p * 2 + (i + 2))
                    dve.wait_ge(sig_ready, n1)
                    dve.wait_ge(g_ready, n1)
                    nc.vector.tensor_tensor(gs, gbuf, sig, ALU.mult).then_inc(gs_ready, 1)
                    dve.wait_ge(gs_ready, n1)
                    dve.wait_ge(gu_read, n1)
                    nc.vector.scalar_tensor_tensor(out=hbuf, in0=ubuf, scalar=1.0, in1=gs,
                                                   op0=ALU.add, op1=ALU.mult).then_inc(h_ready, 1)
                    if first and i == 0:
                        further_blocks()
                    if i == 0:
                        places(S, p + 1, False).then_inc(s_ready, 1)
                    else:
                        places(Sg, p + 1, True).then_inc(sg_ready, 1)
                    dve.wait_ge(y_done, n1)
                    rows = slice(i * CAP, (i + 1) * CAP)
                    nc.vector.tensor_copy(ysb[rows, 0:HALF], xy_ps[0:CAP, :])
                    nc.vector.tensor_copy(ysb[rows, HALF:D], xy_ps[CAP:P, :]).then_inc(y_sb, 1)

            pair(0, first=True)
            with dve.Fori(1, NE // 2) as p:
                pair(p)
            extra = dve.value_load(ctl[0:1, MAXX:MAXX + 1], min_val=0, max_val=MAXX // 2)
            with dve.If(extra > 0):
                with dve.Fori(NE // 2, extra + NE // 2) as p:
                    pair(p)

            for tt in range(TT):
                dve.wait_ge(tile_done, tt + 1)
                for half in range(2):
                    last = nc.vector.bn_stats(stats[:, 2, tt, half, :], acc[tt][half][:, :])
                chain(last)
                nc.vector.bn_aggr(mv[:, 2, tt, :], stats[:, 2, tt, :, :].rearrange("p a b -> p (a b)")).then_inc(var_ready, 1)
                dve.wait_ge(var_ready, TT * 2 + tt + 1)
                dve.wait_ge(std_ready, TT * 2 + tt + 1)
                chain(nc.vector.reciprocal(rstd[:, 2, tt, 1:2], rstd[:, 2, tt, 0:1]))
                nc.vector.tensor_scalar(mv[:, 2, tt, 1:2], mv[:, 2, tt, 0:1], rstd[:, 2, tt, 1:2], -1.0,
                                        ALU.mult, ALU.mult).then_inc(scale_ready, 1)
            dve.wait_ge(ln_in[2], 32)
            for tt in range(TT):
                for half in range(2):
                    cols = slice(half * HALF, (half + 1) * HALF)
                    dve.wait_ge(normed, 2 * tt + half + 1)
                    nc.vector.tensor_tensor(x_nat[:, tt, cols], x_nat[:, tt, cols], lng[:, cols], ALU.mult).then_inc(gained3, 1)
                dve.wait_ge(gained3, 2 * tt + 2)
                nc.vector.tensor_tensor(x_nat[:, tt, HALF:D], x_nat[:, tt, HALF:D], lnb[:, HALF:D],
                                        ALU.add).then_inc(biased_dve, 1)

        @block.tensor
        def _(pe):
            mm = nc.tensor.matmul

            def transposes(src, tag, j):
                name = (tag, j)
                wait_bank(pe, name)
                for tt in range(TT):
                    for a in range(2):
                        k = 2 * j + a
                        last = nc.tensor.transpose(B(name)[:, a * T + tt * P:a * T + (tt + 1) * P],
                                                   src[:, tt, k * P:(k + 1) * P], ident)
                fill(last, name)

            pe.wait_ge(ident_in, 16)
            pe.wait_ge(x_in, 16 * TT)
            for j in range(4):
                transposes(x_nat, "xT", j)
            pe.wait_ge(wf_in, 32)
            name = ("f", 0)
            for k in range(KD):
                if k % 2 == 0:
                    wait_evacuated(pe, ("xT", k // 2))
                last = mm(B(name)[0:NFOX, 0:T], wf[:, k, :], reg_b[:, k, :], start=(k == 0), stop=(k == KD - 1))
            fill(last, name)

            def columns_out(g, j, src, arrived=None):
                w = group_tile(g)
                wait_group(pe, g)
                name = (g, j)
                wait_bank(pe, name)
                for a in range(2):
                    c = (2 * j + a) * P
                    for k in range(KD):
                        if arrived and a == 0:
                            arrived(k)
                        last = mm(B(name)[:, a * T:(a + 1) * T], w[:, k, c:c + P], src[:, k, :],
                                  start=(k == 0), stop=(k == KD - 1))
                fill(last, name)

            def tokens_out(g, tt, src, arrived=None):
                w = group_tile(g)
                wait_group(pe, g)
                name = (g, tt)
                wait_bank(pe, name)
                for k in range(KD):
                    if arrived:
                        arrived(k)
                    last = mm(B(name)[:, :], src[:, k, tt * P:(tt + 1) * P], w[:, k, :],
                              start=(k == 0), stop=(k == KD - 1))
                fill(last, name)

            for j in range(2):
                columns_out("qf", j, reg_b)
            pe.wait_ge(rel_in, 16)
            pe.wait_ge(const_in, 16)
            wait_bank(pe, ("t5", 0))
            fill(mm(B(("t5", 0))[0:NMOBA, 0:3 * P], rel1[:, :], K[0:NBUCKETS + 1, C_T5:C_T5 + 3 * P],
                    start=True, stop=True), ("t5", 0))
            for j in range(2):
                columns_out("kf", j, reg_b)
            pe.wait_ge(mem_in, 16)
            for j in range(4):
                transposes(mem_nat, "mT", j)
            for tt in range(TT):
                tokens_out("vf", tt, reg_b)
            name = ("cT", 0)
            pe.wait_ge(c8_ready, 1)
            wait_bank(pe, name)
            for tt in range(TT):
                last = nc.tensor.transpose(B(name)[:, tt * P:(tt + 1) * P], c8[:, P + tt * P:P + (tt + 1) * P], ident)
            fill(last, name)
            pe.wait_ge(q_zeroed, 1)

            def heads_arrived(k):
                if k == 0 or k == NH // 2 - 1:
                    for i in range(NH // 2 - 1) if k == 0 else (k,):
                        wait_evacuated(pe, ("o", i))

            for what, *item in MIXER:
                if what == "p":
                    g, j = item
                    if g in ("qm", "km"):
                        columns_out(g, j, reg_b)
                    elif g == "vm":
                        tokens_out(g, j, reg_b)
                    elif g[:2] == "ck":
                        if (g, j) == ("ck0", 0):
                            for i in range(4):
                                wait_evacuated(pe, ("mT", i))
                        columns_out(g, j, memT)
                    elif g[:2] == "cv":
                        tokens_out(g, j, memT)
                    else:
                        tokens_out(g, j, oT, heads_arrived if (g, j) == ("wo0", 0) else None)
                    continue
                s = item[0]
                if s < NH:
                    h = s
                    i, e = h // 2, h % 2
                    if h % 4 == 0:
                        fm = "fm"[h // NFOX]
                        for g in ("q" + fm, "k" + fm):
                            wait_evacuated(pe, (g, i % 4 // 2))
                    if h < NFOX:
                        name = ("nc", h)
                        wait_bank(pe, name)
                        fill(mm(B(name)[:, 0:3 * P], ident[:, h:h + 1].to_broadcast([P, P]), c8[:, :],
                                start=True, stop=True), name)
                    name = ("qk", h)
                    wait_bank(pe, name)
                    mm(B(name)[:, 0:P], qpad[:, i, e, 0:P], kT[:, i, 0:P], start=True, stop=True)
                    fill(mm(B(name)[:, P:3 * P], qpad[:, i, e, P:T], kT[:, i, :], start=True, stop=True), name)
                if 0 <= s - 2 < NH:
                    h = s - 2
                    name = ("pt", h)
                    wait_bank(pe, name)
                    pe.wait_ge(probs_ready, h + 1)
                    for a in range(3):
                        last = nc.tensor.transpose(B(name)[:, a * P:(a + 1) * P], L[:, h % 4, a * P:(a + 1) * P], ident)
                    fill(last, name)
                if 0 <= s - 3 < NH:
                    h = s - 3
                    i, e = h // 2, h % 2
                    name = ("o", i)
                    if e == 0:
                        wait_bank(pe, name)
                    if h % NFOX == 0:
                        for tt in range(TT):
                            wait_evacuated(pe, ("v" + "fm"[h // NFOX], tt))
                    wait_evacuated(pe, ("pt", h))
                    rows = slice(e * HD, (e + 1) * HD)
                    cols = slice(h * HD, (h + 1) * HD)
                    mm(B(name)[rows, 0:T], reg_v[:, 0, cols], PT[:, h % 2, 0:T], start=True, stop=False)
                    last = mm(B(name)[rows, P:T], reg_v[:, 1, cols], PT[:, h % 2, T:T + P], start=False, stop=True)
                    if e:
                        fill(last, name)
                    else:
                        last.then_inc(pv_done, 1)

            def transpose_normed(tag, src, i):
                for tt in range(TT):
                    for half in range(2):
                        name = (tag, tt, half)
                        wait_bank(pe, name)
                        pe.wait_ge(xhat_ready, (TT * i + tt) * 2 + half + 1)
                        for j in range(4):
                            k = 4 * half + j
                            last = nc.tensor.transpose(B(name)[:, j * P:(j + 1) * P], src[:, tt, k * P:(k + 1) * P], ident)
                        fill(last, name)

            def normed_arrived(tag):
                def arrived(k):
                    if k % 4 == 0:
                        for tt in range(TT):
                            wait_evacuated(pe, (tag, tt, k // 4))
                return arrived

            transpose_normed("x1T", x1, 0)
            for what, *item in CROSS:
                if what == "p":
                    g, j = item
                    if g == "cv1":
                        tokens_out(g, j, memT)
                    else:
                        columns_out(g, j, reg_b, normed_arrived("x1T") if (g, j) == ("cq0", 0) else None)
                    continue
                s = item[0]
                if s < NCH:
                    name = ("cqk", s)
                    for g in ("cq", "ck"):
                        wait_evacuated(pe, (g + str(s // 2), s % 2))
                    wait_bank(pe, name)
                    for tt in range(TT):
                        for kk in range(2):
                            last = mm(B(name)[:, tt * NMEM:(tt + 1) * NMEM], qcT[:, 2 * s + kk, tt * P:(tt + 1) * P],
                                      kcT[:, 2 * s + kk, :], start=(kk == 0), stop=(kk == 1))
                    fill(last, name)
                if 0 <= s - 1 < NCH:
                    h = s - 1
                    name = ("cpt", h)
                    wait_bank(pe, name)
                    pe.wait_ge(probs_ready, NH + h + 1)
                    for m in range(2):
                        for tt in range(TT):
                            last = nc.tensor.transpose(B(name)[:, m * T + tt * P:m * T + (tt + 1) * P],
                                                       L[:, h % 4, tt * NMEM + m * P:tt * NMEM + (m + 1) * P], ident)
                    fill(last, name)
                if 0 <= s - 2 < NCH:
                    h = s - 2
                    name = ("co", h)
                    wait_bank(pe, name)
                    for tt in range(2):
                        wait_evacuated(pe, (f"cv{h // 2}", tt))
                    wait_evacuated(pe, ("cpt", h))
                    for a in range(2):
                        for m in range(2):
                            last = mm(B(name)[:, a * T:(a + 1) * T], vc[:, m, h * CHD + a * P:h * CHD + (a + 1) * P],
                                      PT[:, h % 2, m * T:(m + 1) * T], start=(m == 0), stop=(m == 1))
                    fill(last, name)

            def cross_arrived(k):
                if k % 2 == 0:
                    wait_evacuated(pe, ("co", k // 2))

            for tt in range(TT):
                for g in ("co0", "co1"):
                    tokens_out(g, tt, ocT, cross_arrived if (g, tt) == ("co0", 0) else None)
            transpose_normed("x2T", x2, 1)

            pe.wait_ge(router_in, 32)
            name = ("rpart", 0)
            wait_bank(pe, name)
            for tt in range(TT):
                for half in range(2):
                    wait_evacuated(pe, ("x2T", tt, half))
            for a in range(2):
                for j in range(4):
                    last = mm(B(name)[j * NE:(j + 1) * NE, 0:T], wr[:, 2 * j + a, :], reg_b[:, 2 * j + a, :],
                              start=(a == 0), stop=(a == 1))
            fill(last, name)
            name = ("router", 0)
            wait_bank(pe, name)
            wait_evacuated(pe, ("rpart", 0))
            for tt in range(TT):
                last = mm(B(name)[:, tt * NE:(tt + 1) * NE], NCt[:, 0, tt * P:(tt + 1) * P], K[:, C_STK:C_STK + NE],
                          start=True, stop=True)
            fill(last, name)
            tri, one = K[:, C_TRI:C_TRI + P], K[:, C_ONE:C_ONE + P]
            name = ("rank", 0)
            wait_bank(pe, name)
            pe.wait_ge(mask_ready, 1)
            mm(B(name)[:, 0:NE], tri, M[:, 0, :], start=True, stop=True)
            mm(B(name)[:, NE:2 * NE], one, M[:, 0, :], start=True, stop=False)
            fill(mm(B(name)[:, NE:2 * NE], tri, M[:, 1, :], start=False, stop=True), name)
            pe.wait_ge(moe_zeroed, 1)
            pe.wait_ge(bgu_in, 16)
            for b in range(8):
                last_job = max(n for n in JOB.values() if n % 8 == b)
                pe.wait_ge(evacuated[b], last_job // 8 + 1)

            def gather(m):
                pe.wait_ge(s_ready, m)
                for half in range(2):
                    dst = (xy_ps, tr_ps)[half]
                    for tt in range(TT):
                        last = mm(dst[:, :], S[:, tt, :], x2[:, tt, half * HALF:(half + 1) * HALF],
                                  start=(tt == 0), stop=(tt == TT - 1))
                    last.then_inc((xg0_done, xg1_done)[half], 1)

            def transpose_xg(half, m):
                pe.wait_ge((xg0_sb, xg1_sb)[half], m)
                for j in range(4):
                    k = 4 * half + j
                    last = nc.tensor.transpose((xy_ps, tr_ps)[half][:, j * P:(j + 1) * P], Xg[:, k * P:(k + 1) * P], ident)
                last.then_inc((xgTa_done, xgTb_done)[half], 1)

            pe.wait_ge(ln_out, 2 * TT)
            gather(1)
            for half in range(2):
                transpose_xg(half, 1)

            def base():
                pe.wait_ge(rep_ready, 1)
                for j in range(2):
                    for tt in range(TT):
                        last = nc.tensor.transpose(xy_ps[0:NQ, j * T + tt * P:j * T + (tt + 1) * P], rep[:, j, tt, :], ident)
                last.then_inc(tab_done, 1)
                for tt in range(TT):
                    for half in range(2):
                        mm(acc[tt][half][:, :], K[:, C_AID:C_AID + P], x2[:, tt, half * HALF:(half + 1) * HALF],
                           start=True, stop=False, skip_group_check=True)
                pe.wait_ge(cand_ready, 1)
                mm(xy_ps[0:NQ, 0:1], K[0:NQ, C_STR:C_STR + NQ], cand[:, 1:2], start=True, stop=True).then_inc(pos_done, 1)
                pe.wait_ge(bdn_in, 16)
                pe.wait_ge(tab_sb, 1)
                for tt in range(TT):
                    for half in range(2):
                        mm(acc[tt][half][:, :], repT[:, 1, tt * P:(tt + 1) * P], bdn[0:NQ, half * HALF:(half + 1) * HALF],
                           start=False, stop=False, skip_group_check=True)
                pe.wait_ge(pq_ready, 1)
                for j in range(2):
                    for tt in range(TT):
                        c = (2 * j + tt) * MAXX
                        mm(xy_ps[:, c:c + MAXX], repT[:, j, tt * P:(tt + 1) * P], Pq[:, :], start=True, stop=True)
                mm(xy_ps[:, 4 * MAXX:5 * MAXX], K[0:NQ, C_SEL:C_SEL + P], Pq[:, :], start=True, stop=True)
                mm(xy_ps[0:1, 5 * MAXX:6 * MAXX], K[0:NQ, C_EID:C_EID + 1], Pq[:, :], start=True, stop=True)
                mm(xy_ps[0:1, 6 * MAXX:6 * MAXX + 1], K[0:NQ, C_ONE:C_ONE + 1], cand[:, 1:2],
                   start=True, stop=True).then_inc(over_done, 1)

            def scatter(tt):
                for half in range(2):
                    last = mm(acc[tt][half][:, :], SgT[:, tt * P:(tt + 1) * P], ysb[:, half * HALF:(half + 1) * HALF],
                              start=False, stop=False, skip_group_check=True)
                return last

            def gate_up(p, i, first):
                n = p * 2 + i
                if not (first and i == 0):
                    pe.wait_ge(gu_read, n)
                pe.wait_ge(bsel_ready, n + 1)
                for ps, c0 in ((gate_ps, 0), (up_ps, F)):
                    for half in range(2):
                        c = c0 + half * HALF
                        mm(ps[half * CAP:(half + 1) * CAP, :], bsel[:, i, :], bgu[:, c:c + HALF], start=True, stop=False)
                if i == 0:
                    pe.wait_ge(xgTa_sb, p + 1)
                for k in range(KD):
                    if i == 0 and k == KD // 2:
                        pe.wait_ge(xgTb_sb, p + 1)
                    pe.wait_ge(chunk_in[k], n * 16 + 16)
                    w = chunk_tile(k, i if first else None)
                    for ps, c0 in ((gate_ps, 0), (up_ps, F)):
                        for half in range(2):
                            c = c0 + half * HALF
                            last = mm(ps[half * CAP:(half + 1) * CAP, :], xgT[:, k, i * CAP:(i + 1) * CAP],
                                      w[:, c:c + HALF], start=False, stop=(k == KD - 1))
                    if k < KD - 1:
                        last.then_inc(chunks_used, 1)
                last.then_inc(gu_done, 1)

            def transpose_h(n1):
                pe.wait_ge(h_ready, n1)
                for j in range(4):
                    last = nc.tensor.transpose(tr_ps[:, j * P:(j + 1) * P], hbuf[:, j * P:(j + 1) * P], ident)
                last.then_inc(hT_done, 1)

            def down(p, i, ks, first):
                for k in ks:
                    c, j = GUC + k // 2, k % 2
                    if j == 0:
                        pe.wait_ge(chunk_in[c], (p * 2 + i) * 16 + 16)
                    w = chunk_tile(c, i if first else None)
                    a = (k % 4) * P + (k // 4) * CAP
                    for half in range(2):
                        last = mm(xy_ps[half * CAP:(half + 1) * CAP, :], hT[:, a:a + CAP],
                                  w[:, j, half * HALF:(half + 1) * HALF], start=(k == 0), stop=(k == KD - 1))
                    if j and k < KD - 1:
                        last.then_inc(chunks_used, 1)
                if k == KD - 1:
                    last.then_inc(y_done, 1)

            def pair(p, first=False):
                gate_up(p, 0, first)
                if first:
                    base()
                else:
                    pe.wait_ge(y_sb, p * 2)
                    pe.wait_ge(sgT_sb, p)
                    scatter(0)
                    scatter(1).then_inc(scattered, 1)
                pe.wait_ge(sg_ready, p + 1)
                pe.wait_ge(xgTb_sb, p + 1)
                for tt in range(TT):
                    last = nc.tensor.transpose(tr_ps[:, tt * P:(tt + 1) * P], Sg[:, tt, :], ident)
                last.then_inc(sgT_done, 1)
                pe.wait_ge(sgT_sb, p + 1)
                transpose_h(p * 2 + 1)
                pe.wait_ge(hT_sb, p * 2 + 1)
                if first:
                    pe.wait_ge(tables_ready, 1)
                down(p, 0, range(KD), first)
                gate_up(p, 1, first)
                pe.wait_ge(y_sb, p * 2 + 1)
                gather(p + 2)
                pe.wait_ge(xg1_sb, p + 2)
                transpose_h(p * 2 + 2)
                transpose_xg(0, p + 2)
                pe.wait_ge(hT_sb, p * 2 + 2)
                pe.wait_ge(xgTa_sb, p + 2)
                down(p, 1, range(KD // 2), first)
                transpose_xg(1, p + 2)
                down(p, 1, range(KD // 2, KD), first)

            pair(0, first=True)
            with pe.Fori(1, NE // 2) as p:
                pair(p)
            pe.wait_ge(tables_ready, 1)
            extra = pe.value_load(ctl[0:1, MAXX:MAXX + 1], min_val=0, max_val=MAXX // 2)
            with pe.If(extra > 0):
                with pe.Fori(NE // 2, extra + NE // 2) as p:
                    pair(p)
            pe.wait_ge(y_sb, extra * 2 + NE)
            pe.wait_ge(sgT_sb, extra + NE // 2)
            for tt in range(TT):
                scatter(tt).then_inc(tile_done, 1)


INS = ["x", "mem", "w_in", "b_forget", "w_mix_out", "rel_bias", "ln1_g", "ln1_b", "w_cq", "w_ck", "w_cv", "w_co",
       "ln2_g", "ln2_b", "w_router", "b_router", "w_gate_up", "b_gate_up", "w_down", "b_down", "ln3_g", "ln3_b"]


def kernel(**inputs):
    import concourse.bacc as bacc
    from concourse.bass_utils import run_bass_kernel_spmd

    nc = bacc.Bacc("TRN2", target_bir_lowering=False, num_devices=1)
    arrays = {f"in_{n}": np.ascontiguousarray(inputs[n]) for n in INS}
    arrays["in_consts"] = constants()
    args = [nc.dram_tensor(n, a.shape, mybir.dt.from_np(a.dtype), kind="ExternalInput").ap() for n, a in arrays.items()]
    out = nc.dram_tensor("out", (1, T, D), mybir.dt.float32, kind="ExternalOutput").ap()
    hybrid_layer(nc, *args, out)
    r = run_bass_kernel_spmd(nc, [arrays], core_ids=[0])
    return r.results[0]["out"]
```
